# Optimizing a Trainium2 kernel written in Bass

```python
import math
import jax
import jax.numpy as jnp
from jax import lax
import numpy as np

D_MODEL = 1024
BATCH = 1
SEQ = 512
DEPTH = 2

GRID_W = 64
CTX_LEN = 256
EPS = 1e-6

SSD_HEADS = 6
SSD_HEAD_DIM = 64
SSD_INNER = SSD_HEADS * SSD_HEAD_DIM
SSD_GROUPS = 2
SSD_STATE = 128
SSD_CONV = 4
SSD_CHUNK = 128
XBC_DIM = SSD_INNER + 2 * SSD_GROUPS * SSD_STATE

MLA_HEADS = 6
Q_LORA = 256
KV_LORA = 256
QK_NOPE = 64
QK_ROPE = 32
V_HEAD = 64
QK_DIM = QK_NOPE + QK_ROPE
MLA_OUT = MLA_HEADS * V_HEAD
ROPE_THETA = 10000.0
ROPE_PAIRS = QK_ROPE // 4
Q_BLOCK = 128

POOL_WINDOWS = (2, 4, 8, 16)
POOL_GROUPS = len(POOL_WINDOWS)
POOL_GROUP_DIM = 64
POOL_DIM = POOL_GROUPS * POOL_GROUP_DIM

MIX_DIM = SSD_INNER + MLA_OUT + POOL_DIM
D_FF = 4 * D_MODEL

OFF_Z = 0
OFF_XBC = OFF_Z + SSD_INNER
OFF_DT = OFF_XBC + XBC_DIM
OFF_QA = OFF_DT + 2 * SSD_HEADS
OFF_KVA = OFF_QA + Q_LORA
OFF_KROPE = OFF_KVA + KV_LORA
OFF_POOL = OFF_KROPE + QK_ROPE
IN_COLS = OFF_POOL + POOL_DIM

kernel_name = "hybrid_ssd_mla_pool_diffusion_block"

def rmsnorm(u, w):
    uf = u.astype(jnp.float32)
    y = uf * lax.rsqrt(jnp.mean(uf * uf, axis=-1, keepdims=True) + EPS)
    return (y * w.astype(jnp.float32)).astype(u.dtype)

def adaln(cond, mod_w, mod_b):
    m = jax.nn.silu(cond) @ mod_w + mod_b
    return jnp.split(m[..., None, :], 6, axis=-1)

def modulate(h, shift, scale):
    return h * (1.0 + scale) + shift

def squared_relu_mlp(h, w1, w2):
    return jnp.square(jax.nn.relu(h @ w1)) @ w2

def axial_rope_tables(n):
    rows = n // GRID_W
    row = jnp.repeat(jnp.arange(rows, dtype=jnp.float32), GRID_W)
    col = jnp.tile(jnp.arange(GRID_W, dtype=jnp.float32), rows)
    inv_freq = ROPE_THETA ** (-jnp.arange(ROPE_PAIRS, dtype=jnp.float32) / ROPE_PAIRS)
    ang = jnp.stack([row[:, None] * inv_freq, col[:, None] * inv_freq], axis=1)
    return jnp.cos(ang), jnp.sin(ang)

def apply_axial_rope(u, cos, sin):
    shp = u.shape
    ur = u.astype(jnp.float32).reshape(shp[:-1] + (2, 2, ROPE_PAIRS))
    u1, u2 = ur[..., 0, :], ur[..., 1, :]
    bshape = (shp[1],) + (1,) * (u.ndim - 3) + (2, ROPE_PAIRS)
    cos = cos.reshape(bshape)
    sin = sin.reshape(bshape)
    out = jnp.stack([u1 * cos - u2 * sin, u2 * cos + u1 * sin], axis=-2)
    return out.reshape(shp).astype(u.dtype)

def depthwise_conv_centred(u, w, b):
    k = w.shape[0]
    out = lax.conv_general_dilated(u, w[:, None, :].astype(u.dtype), (1,), [((k - 1) // 2, k // 2)],
                                   dimension_numbers=('NWC', 'WIO', 'NWC'),
                                   feature_group_count=u.shape[-1])
    return out + b

def ssd_inputs(proj, conv_w, conv_b, dt_bias):
    bsz, n = proj.shape[:2]
    z = proj[..., OFF_Z:OFF_XBC]
    xbc = jax.nn.silu(depthwise_conv_centred(proj[..., OFF_XBC:OFF_DT], conv_w, conv_b))
    xs = xbc[..., :SSD_INNER].reshape(bsz, n, SSD_HEADS, SSD_HEAD_DIM)
    bm = xbc[..., SSD_INNER:SSD_INNER + SSD_GROUPS * SSD_STATE].reshape(bsz, n, SSD_GROUPS, SSD_STATE)
    cm = xbc[..., SSD_INNER + SSD_GROUPS * SSD_STATE:].reshape(bsz, n, SSD_GROUPS, SSD_STATE)
    dt_raw = proj[..., OFF_DT:OFF_QA].astype(jnp.float32).reshape(bsz, n, 2, SSD_HEADS)
    dt = jax.nn.softplus(dt_raw + dt_bias.astype(jnp.float32))
    return z, xs, bm, cm, dt

def segsum_exp(a):
    l = a.shape[-1]
    cs = jnp.cumsum(a, axis=-1)
    diff = cs[..., :, None] - cs[..., None, :]
    mask = jnp.tril(jnp.ones((l, l), dtype=bool))
    return jnp.exp(jnp.where(mask, diff, -jnp.inf))

def ssd_chunked_scan(xs, dt, a, b_mat, c_mat, h0):
    f32 = jnp.float32
    bsz, n = xs.shape[:2]
    nc = n // SSD_CHUNK
    r = SSD_HEADS // SSD_GROUPS
    dt = dt.astype(f32)
    x = (xs.astype(f32) * dt[..., None]).reshape(bsz, nc, SSD_CHUNK, SSD_GROUPS, r, SSD_HEAD_DIM)
    adt = jnp.moveaxis((dt * a.astype(f32)).reshape(bsz, nc, SSD_CHUNK, SSD_GROUPS, r), 2, -1)
    bm = b_mat.astype(f32).reshape(bsz, nc, SSD_CHUNK, SSD_GROUPS, SSD_STATE)
    cm = c_mat.astype(f32).reshape(bsz, nc, SSD_CHUNK, SSD_GROUPS, SSD_STATE)
    a_cs = jnp.cumsum(adt, axis=-1)
    l_mat = segsum_exp(adt)
    cb = jnp.einsum('bclgn,bcsgn->bcgls', cm, bm)
    y_diag = jnp.einsum('bcgrls,bcsgrp->bclgrp', cb[:, :, :, None] * l_mat, x)
    decay_to_end = jnp.exp(a_cs[..., -1:] - a_cs)
    chunk_states = jnp.einsum('bclgn,bcgrl,bclgrp->bcgrpn', bm, decay_to_end, x)
    chunk_decay = jnp.exp(a_cs[..., -1])

    def carry_step(h, inp):
        s_c, d_c = inp
        return h * d_c[..., None, None] + s_c, h

    h_init = h0.astype(f32).reshape(bsz, SSD_GROUPS, r, SSD_HEAD_DIM, SSD_STATE)
    h_last, h_in = lax.scan(carry_step, h_init,
                            (jnp.moveaxis(chunk_states, 1, 0), jnp.moveaxis(chunk_decay, 1, 0)))
    h_in = jnp.moveaxis(h_in, 0, 1)
    y_off = jnp.einsum('bclgn,bcgrpn,bcgrl->bclgrp', cm, h_in, jnp.exp(a_cs))
    y = (y_diag + y_off).reshape(bsz, n, SSD_HEADS, SSD_HEAD_DIM)
    return y, h_last.reshape(bsz, SSD_HEADS, SSD_HEAD_DIM, SSD_STATE)

def ssd_bidirectional(xs, bm, cm, dt, a, h0_fwd, h0_bwd):
    flip = lambda t: jnp.flip(t, axis=1)
    y_f, h_f = ssd_chunked_scan(xs, dt[:, :, 0], a[0], bm, cm, h0_fwd)
    y_b, h_b = ssd_chunked_scan(flip(xs), flip(dt[:, :, 1]), a[1], flip(bm), flip(cm), h0_bwd)
    return y_f + flip(y_b), h_f, h_b

def ssd_output(y, xs, z, d_skip, norm_w):
    bsz, n = y.shape[:2]
    y = y + xs.astype(jnp.float32) * d_skip.astype(jnp.float32)[:, None]
    g = (y.reshape(bsz, n, SSD_INNER) * jax.nn.silu(z.astype(jnp.float32)))
    g = g.reshape(bsz, n, SSD_GROUPS, SSD_INNER // SSD_GROUPS)
    g = g * lax.rsqrt(jnp.mean(g * g, axis=-1, keepdims=True) + EPS)
    return (g.reshape(bsz, n, SSD_INNER) * norm_w.astype(jnp.float32)).astype(z.dtype)

def mla_qkv(proj, q_a_norm_w, w_q_b, kv_a_norm_w, w_kv_b, rope):
    bsz, n = proj.shape[:2]
    cq = rmsnorm(proj[..., OFF_QA:OFF_KVA], q_a_norm_w)
    q = (cq @ w_q_b).reshape(bsz, n, MLA_HEADS, QK_DIM)
    ckv = rmsnorm(proj[..., OFF_KVA:OFF_KROPE], kv_a_norm_w)
    k_rope = proj[..., OFF_KROPE:OFF_POOL]
    kv = (ckv @ w_kv_b).reshape(bsz, n, MLA_HEADS, QK_NOPE + V_HEAD)
    k_nope, v = kv[..., :QK_NOPE], kv[..., QK_NOPE:]
    q_nope, q_rope = q[..., :QK_NOPE], q[..., QK_NOPE:]
    if rope is not None:
        cos, sin = rope
        q_rope = apply_axial_rope(q_rope, cos, sin)
        k_rope = apply_axial_rope(k_rope, cos, sin)
    q = jnp.concatenate([q_nope, q_rope], axis=-1)
    k = jnp.concatenate([k_nope, jnp.broadcast_to(k_rope[:, :, None, :], (bsz, n, MLA_HEADS, QK_ROPE))], axis=-1)
    return q, k, v

def attend(q, k, v):
    s = jnp.einsum('bqhd,bkhd->bhqk', q, k, preferred_element_type=jnp.float32) * (QK_DIM ** -0.5)
    p = jax.nn.softmax(s, axis=-1).astype(v.dtype)
    return jnp.einsum('bhqk,bkhd->bqhd', p, v)

def attend_blocked(q, k, v):
    bsz, n, h, dq = q.shape
    qb = jnp.moveaxis(q.reshape(bsz, n // Q_BLOCK, Q_BLOCK, h, dq), 1, 0)
    out = lax.map(lambda qi: attend(qi, k, v), qb)
    return jnp.moveaxis(out, 0, 1).reshape(bsz, n, h, v.shape[-1])

def multiscale_pool(u, pool_w, pool_scale):
    bsz, n, _ = u.shape
    uf = u.astype(jnp.float32)
    cs = jnp.pad(jnp.cumsum(uf, axis=1), ((0, 0), (1, 0), (0, 0)))
    t = jnp.arange(n)
    outs = []
    for gi, w in enumerate(POOL_WINDOWS):
        sl = slice(gi * POOL_GROUP_DIM, (gi + 1) * POOL_GROUP_DIM)
        lo = jnp.clip(t - w // 2, 0, n)
        hi = jnp.clip(t + w - w // 2, 0, n)
        csg = cs[..., sl]
        mean = (jnp.take(csg, hi, axis=1) - jnp.take(csg, lo, axis=1)) / (hi - lo).astype(jnp.float32)[:, None]
        outs.append(mean - uf[..., sl])
    d = jnp.stack(outs, axis=2)
    y = jnp.einsum('blgc,gcd->blgd', d, pool_w.astype(jnp.float32)).reshape(bsz, n, POOL_DIM)
    return (y * pool_scale.astype(jnp.float32)).astype(u.dtype)

def hybrid_layer(x, ctx, c, c_ctx, rope, mod_w, mod_b, norm1_w, norm2_w, w_in, conv_w, conv_b,
                 dt_bias, a_log, ssd_d, ssd_norm_w, q_a_norm_w, w_q_b, kv_a_norm_w, w_kv_b,
                 pool_w, pool_scale, w_out, w_mlp1, w_mlp2, update_ctx):
    bsz, n, _ = x.shape
    m = ctx.shape[1]
    sh1, sc1, g1, sh2, sc2, g2 = adaln(c, mod_w, mod_b)
    csh1, csc1, cg1, csh2, csc2, cg2 = adaln(c_ctx, mod_w, mod_b)
    px = modulate(rmsnorm(x, norm1_w), sh1, sc1) @ w_in
    pc = modulate(rmsnorm(ctx, norm1_w), csh1, csc1) @ w_in

    a = -jnp.exp(a_log.astype(jnp.float32))
    zc, xsc, bmc, cmc, dtc = ssd_inputs(pc, conv_w, conv_b, dt_bias)
    zx, xsx, bmx, cmx, dtx = ssd_inputs(px, conv_w, conv_b, dt_bias)
    h_zero = jnp.zeros((bsz, SSD_HEADS, SSD_HEAD_DIM, SSD_STATE), jnp.float32)
    yc, hf_ctx, hb_ctx = ssd_bidirectional(xsc, bmc, cmc, dtc, a, h_zero, h_zero)
    yx, _, _ = ssd_bidirectional(xsx, bmx, cmx, dtx, a, hf_ctx, hb_ctx)
    ssd_x = ssd_output(yx, xsx, zx, ssd_d, ssd_norm_w)

    qc, kc, vc = mla_qkv(pc, q_a_norm_w, w_q_b, kv_a_norm_w, w_kv_b, None)
    qx, kx, vx = mla_qkv(px, q_a_norm_w, w_q_b, kv_a_norm_w, w_kv_b, rope)
    attn_x = attend_blocked(qx, jnp.concatenate([kx, kc], axis=1), jnp.concatenate([vx, vc], axis=1))

    pool_x = multiscale_pool(px[..., OFF_POOL:], pool_w, pool_scale)

    mix_x = jnp.concatenate([ssd_x, attn_x.reshape(bsz, n, MLA_OUT), pool_x], axis=-1) @ w_out
    x = x + g1 * mix_x
    x = x + g2 * squared_relu_mlp(modulate(rmsnorm(x, norm2_w), sh2, sc2), w_mlp1, w_mlp2)

    if update_ctx:
        ssd_c = ssd_output(yc, xsc, zc, ssd_d, ssd_norm_w)
        attn_c = attend(qc, kc, vc).reshape(bsz, m, MLA_OUT)
        pool_c = multiscale_pool(pc[..., OFF_POOL:], pool_w, pool_scale)
        mix_c = jnp.concatenate([ssd_c, attn_c, pool_c], axis=-1) @ w_out
        ctx = ctx + cg1 * mix_c
        ctx = ctx + cg2 * squared_relu_mlp(modulate(rmsnorm(ctx, norm2_w), csh2, csc2), w_mlp1, w_mlp2)
    return x, ctx

def setup_inputs(seed: int = 0) -> dict:
    key = jax.random.key(seed)
    ks = jax.random.split(key, 32)
    f32 = jnp.float32

    def nrm(k, shape, scale):
        return jax.random.normal(k, shape, f32) * scale

    def gain(k, shape):
        return 1.0 + 0.02 * jax.random.normal(k, shape, f32)

    dt0 = jnp.exp(jax.random.uniform(ks[11], (DEPTH, 2, SSD_HEADS), f32, math.log(1e-3), math.log(1e-1)))
    return {
        "x": nrm(ks[0], (BATCH, SEQ, D_MODEL), 1.0),
        "c": nrm(ks[1], (BATCH, D_MODEL), 1.0),
        "ctx": nrm(ks[2], (BATCH, CTX_LEN, D_MODEL), 1.0),
        "c_ctx": nrm(ks[3], (D_MODEL,), 1.0),
        "mod_w": nrm(ks[4], (DEPTH, D_MODEL, 6 * D_MODEL), 0.5 * D_MODEL ** -0.5),
        "mod_b": nrm(ks[5], (DEPTH, 6 * D_MODEL), 0.01),
        "norm1_w": gain(ks[6], (DEPTH, D_MODEL)),
        "norm2_w": gain(ks[7], (DEPTH, D_MODEL)),
        "w_in": nrm(ks[8], (DEPTH, D_MODEL, IN_COLS), D_MODEL ** -0.5),
        "conv_w": nrm(ks[9], (DEPTH, SSD_CONV, XBC_DIM), SSD_CONV ** -0.5),
        "conv_b": nrm(ks[10], (DEPTH, XBC_DIM), 0.01),
        "dt_bias": dt0 + jnp.log(-jnp.expm1(-dt0)),
        "a_log": jnp.log(jax.random.uniform(ks[12], (DEPTH, 2, SSD_HEADS), f32, 1.0, 16.0)),
        "ssd_d": 1.0 + 0.1 * jax.random.normal(ks[13], (DEPTH, SSD_HEADS), f32),
        "ssd_norm_w": gain(ks[14], (DEPTH, SSD_INNER)),
        "q_a_norm_w": gain(ks[15], (DEPTH, Q_LORA)),
        "w_q_b": nrm(ks[16], (DEPTH, Q_LORA, MLA_HEADS * QK_DIM), Q_LORA ** -0.5),
        "kv_a_norm_w": gain(ks[17], (DEPTH, KV_LORA)),
        "w_kv_b": nrm(ks[18], (DEPTH, KV_LORA, MLA_HEADS * (QK_NOPE + V_HEAD)), KV_LORA ** -0.5),
        "pool_w": nrm(ks[19], (DEPTH, POOL_GROUPS, POOL_GROUP_DIM, POOL_GROUP_DIM), POOL_GROUP_DIM ** -0.5),
        "pool_scale": gain(ks[20], (DEPTH, POOL_DIM)),
        "w_out": nrm(ks[21], (DEPTH, MIX_DIM, D_MODEL), MIX_DIM ** -0.5),
        "w_mlp1": nrm(ks[22], (DEPTH, D_MODEL, D_FF), D_MODEL ** -0.5),
        "w_mlp2": nrm(ks[23], (DEPTH, D_FF, D_MODEL), D_FF ** -0.5),
        "final_norm_w": gain(ks[24], (D_MODEL,)),
    }

def reference(x, c, ctx, c_ctx, mod_w, mod_b, norm1_w, norm2_w, w_in, conv_w, conv_b, dt_bias, a_log,
              ssd_d, ssd_norm_w, q_a_norm_w, w_q_b, kv_a_norm_w, w_kv_b, pool_w, pool_scale, w_out,
              w_mlp1, w_mlp2, final_norm_w):
    rope = axial_rope_tables(x.shape[1])
    for i in range(DEPTH):
        x, ctx = hybrid_layer(x, ctx, c, c_ctx, rope, mod_w[i], mod_b[i], norm1_w[i], norm2_w[i], w_in[i],
                              conv_w[i], conv_b[i], dt_bias[i], a_log[i], ssd_d[i], ssd_norm_w[i],
                              q_a_norm_w[i], w_q_b[i], kv_a_norm_w[i], w_kv_b[i], pool_w[i], pool_scale[i],
                              w_out[i], w_mlp1[i], w_mlp2[i], update_ctx=(i < DEPTH - 1))
    return rmsnorm(x, final_norm_w)


_drawn_inputs = setup_inputs


def setup_inputs(seed=0):
    import zlib

    import numpy as np

    out = dict(_drawn_inputs(seed))
    spreads = {}
    factors = {'ctx': 4.965,
     'norm1_w': 6.753,
     'norm2_w': 4.511,
     'conv_b': 64.0,
     'ssd_d': 64.0,
     'ssd_norm_w': 51.283,
     'q_a_norm_w': 8.0,
     'w_q_b': 2.685,
     'kv_a_norm_w': 8.0,
     'pool_scale': 8.0,
     'final_norm_w': 8.204}
    for name, (base, spread) in spreads.items():
        noise = np.random.default_rng([zlib.crc32(name.encode()), seed]).standard_normal(out[name].shape)
        drawn = base * np.exp(spread * noise) if base else spread * noise
        out[name] = jnp.asarray(drawn.astype(out[name].dtype))
    for name, factor in factors.items():
        out[name] = (out[name] * factor).astype(out[name].dtype)
    return out
```

```python
from contextlib import ExitStack

import concourse.bass as bass
from concourse import mybir

F32 = mybir.dt.float32
F32R = mybir.dt.float32r
BF16 = mybir.dt.bfloat16
ALU = mybir.AluOpType
ACT = mybir.ActivationFunctionType
AX = mybir.AxisListType

P = 128
D_MODEL, SEQ, CTX_LEN, DEPTH = 1024, 512, 256, 2
T = SEQ + CTX_LEN
KB = D_MODEL // P
EPS = 1e-6
HEADS, HD, GROUPS, STATE = 6, 64, 2, 128
INNER = HEADS * HD
GH = HEADS // GROUPS
GW = GH * HD
QK_NOPE, QK_ROPE, V_HEAD = 64, 32, 64
QK_DIM = QK_NOPE + QK_ROPE
LORA = 256
D_FF = 4 * D_MODEL
NCH = T // P
XCH = SEQ // P

GAP = 8
XO = GAP
CO = GAP + SEQ + GAP
ROW = CO + CTX_LEN + GAP
SPAN = CO + CTX_LEN - XO

B_MISC, B_KVA, B_XS, B_B, B_C, B_QA, B_Z, B_POOL = 0, 1, 3, 6, 8, 10, 12, 15
NBLK = 17
CTX_BLOCKS = B_C
B_ATT = B_KVA

IN_PANELS, OUT_PANELS, FF_GROUPS = NBLK, KB, 4
LAYER_PANELS = IN_PANELS + OUT_PANELS + FF_GROUPS * 2 * KB
MOD_PANELS = 6 * KB
SH1, SC1, G1, SH2, SC2, G2 = range(6)
MOD_EARLY = KB
MOD_START = KB
MOD_IN = IN_PANELS + 1
MOD_OUT = 2 * (OUT_PANELS - 1)
MOD_PER_GROUP = MOD_PANELS // FF_GROUPS
FIRST_IN = MOD_START
FIRST_OUT = FIRST_IN + MOD_IN
FIRST_MLP = FIRST_OUT + MOD_OUT

PV = {}
_at = 0
for _name, _n in (("mod_b", 48), ("norm1", 8), ("norm2", 8), ("conv_w", 28), ("conv_b", 7), ("ssd_norm", 3),
                  ("qa_norm", 2), ("kva_norm", 2), ("pool_scale", 2), ("dt_bias", 12), ("a_log", 12), ("ssd_d", 6)):
    PV[_name] = (_at, _at + _n)
    _at += _n
NPV = _at
CV = {}
_at = 0
for _name, _n in (("ident", 128), ("from", 128), ("upto", 128), ("ones", 128), ("cos", 512),
                  ("sin", 512), ("rw", 2), ("edge", 32)):
    CV[_name] = (_at, _at + _n)
    _at += _n
NCV = _at


def part_columns(part):
    return ((0, SEQ), (XO, XO + SEQ)) if part == 0 else ((SEQ, T), (CO, CO + CTX_LEN))


def chunk_at(c):
    return XO + P * c if c < XCH else CO + P * (c - XCH)


def build(nc, panels, mod_early, mod_late, x_in, cond_in, cond_rows, params, final_w, consts, masks, wqb_in, wkvb_in,
          poolw_in, out):
    ctx = ExitStack()
    with ctx:
        taken = {}

        def sb(name, shape, dt, offset, size=4):
            n = size
            for s in shape[1:]:
                n *= s
            taken[name] = (offset, n)
            return nc.alloc_sbuf_tensor_at(name, shape, dt, offset=offset), offset + (n + 31) // 32 * 32

        base = 16512
        xres, at = sb("xres", [P, KB, T], F32, base)
        act_base = at
        mod_raw, _ = sb("mod_raw", [P, MOD_EARLY, KB, P], F32, at)
        act_hi, at = sb("act_hi", [P, KB, T], F32R, at)
        act_lo, at = sb("act_lo", [P, KB, T], F32R, at)
        act_end = at
        h_hi, h_at = sb("h_hi", [P, KB, T], F32R, at)
        h_lo, h_end = sb("h_lo", [P, KB, T], F32R, h_at)
        proj, at = sb("proj", [P, NBLK, ROW], F32, at)
        assert h_end <= at
        w_raw, at = sb("w_raw", [P, 2, KB, P], F32, at)
        w_hi, at = sb("w_hi", [P, 2, KB, P], F32R, at)
        w_lo, at = sb("w_lo", [P, 2, KB, P], F32R, at)
        pool_a, a2 = sb("pool_a", [P, ROW], F32, at)
        pool_b, a2 = sb("pool_b", [P, ROW], F32, a2)
        mod_rows, at = sb("mod_rows", [P, 2, D_MODEL], F32, at)
        assert a2 <= at
        cst, at = sb("cst", [P, NCV], F32, at)
        msk, at = sb("msk", [P, 3, P], BF16, at, 2)
        par, at = sb("par", [P, DEPTH, NPV], F32, at)
        fin_w, at = sb("fin_w", [P, KB], F32, at)
        cond, at = sb("cond", [P, KB, 2], F32, at)
        eps, at = sb("eps", [P, 1], F32, at)
        a_exp, at = sb("a_exp", [P, DEPTH, 2 * HEADS], F32, at)
        modv, at = sb("modv", [P, DEPTH, 6 * KB, 2], F32, at)
        gain, at = sb("gain", [P, KB, 2], F32, at)
        wkvb, at = sb("wkvb", [P, 2, HEADS * P], F32, at)
        poolw, at = sb("poolw", [P, 2, P], F32, at)
        rstd, at = sb("rstd", [P, T], F32, at)
        s0 = at
        sq, a1 = sb("sq", [P, 2, T], F32, s0)
        tmp, a1 = sb("tmp", [P, 2, T], F32, a1)
        tok, at = sb("tok", [P, NCH, 5 * P], F32, s0)
        hf, at = sb("hf", [P, INNER], F32, at)
        xw, at = sb("xw", [P, INNER], F32, at)
        wide, a3 = sb("wide", [P, 2, ROW], F32, at)
        E, at = sb("E", [P, 2, GH * P], F32, at)
        M, at = sb("M", [P, 2, 2, GH * P], F32, at)
        assert a3 <= at and a1 <= at
        cond_b, a4 = sb("cond_b", [P, 2, D_MODEL], F32, a3)
        ytok, at = sb("ytok", [P, INNER], F32, at)
        assert a4 <= 229344, a4
        assert at <= 229344, at
        at = act_base
        qT, at = sb("qT", [P, 2, T], F32, at)
        kT, at = sb("kT", [P, 2, T], F32, at)
        vtok, at = sb("vtok", [P, NCH, INNER], F32, at)
        Pm, at = sb("Pm", [P, 2, T], F32, at)
        PT, at = sb("PT", [P, NCH, P], F32, at)
        wqb, at = sb("wqb", [P, 2, HEADS * P], F32, at)
        sm, at = sb("sm", [P, 2, 4], F32, at)
        DTN = NCH * 2 * HEADS
        dts, at = sb("dts", [P, 10, DTN], F32, at)
        ao, at = sb("ao", [P, NCH, INNER], F32, at)
        assert at <= act_end, (at, act_end)

        g = [ctx.enter_context(nc.psum_tensor(f"g{i}", [P, 1024], F32)) for i in range(2)]
        m01 = ctx.enter_context(nc.psum_tensor("m01", [P, 1024], F32))
        pair = ctx.enter_context(nc.psum_tensor("pair", [P, 1024], F32))
        pd, pmod = pair[:, 0:512], pair[:, 512:1024]

        def sem(name):
            return ctx.enter_context(nc.semaphore(name))

        const_loaded = sem("const_loaded")
        x_loaded = sem("x_loaded")
        raw_loaded = [sem(f"raw_loaded{i}") for i in range(2)]
        mod_loaded = [sem(f"mod_loaded{i}") for i in range(2)]
        early_loaded = [sem(f"early_loaded{i}") for i in range(2)]
        hi_ready, lo_ready, panel_used, psum_free = (sem(n) for n in ("hi_ready", "lo_ready", "panel_used", "psum_free"))
        ctx_free = sem("ctx_free")
        mod_used, cond_ready, out_stored = sem("mod_used"), sem("cond_ready"), sem("out_stored")
        mod_step, cond_loaded = sem("mod_step"), sem("cond_loaded")
        relu_ready, hid_ready, hid_hi, hid_lo = (sem(n) for n in ("relu_ready", "hid_ready", "hid_hi", "hid_lo"))
        dve_chain, act_chain, pool_chain = sem("dve_chain"), sem("act_chain"), sem("pool_chain")
        sq_ready, sq_added, sum_ready, rstd_ready, scaled, norm_hi, norm_lo = (
            sem(n) for n in ("sq_ready", "sq_added", "sum_ready", "rstd_ready", "scaled", "norm_hi", "norm_lo"))
        mod_ready, ctx_scaled, ctx_lo = (sem(n) for n in ("mod_ready", "ctx_scaled", "ctx_lo"))
        added = {"conv_pre": 7, "conv_acc": 7, "z_done": 3, "dt_tp": 1, "dt_pre": 1, "dt_exp": 2, "cs_ready": 1, "cs_exp": 3,
                 "cs_neg": 1, "adt_ready": 1, "csq_ready": 2, "csum_ready": 2, "tok_tp": NCH, "v_ready": NCH}
        both_layers = {n: sem(n) for n in added}

        def before(L, name):
            return L * added[name]

        names = ("gaps_zero", "conv_done", "tok_ready", "xw_ready", "st_ready", "hb_ready", "hf_ready", "cb_ready",
                 "r_ready", "e_ready", "m_ready", "m_used", "yoff_ready", "ytok_ready", "yt_ready", "gated",
                 "crstd_ready", "code_ready", "gsq_ready", "gsq_added", "gsum_ready", "grstd_ready", "ssd_done",
                 "v_done", "swapped", "kr_done", "kr_rows", "q_ready", "m_sum",
                 "rope_done", "k_ready", "k_copied", "s_ready", "max_ready", "p_ready", "pt_ready", "pt_act", "pt_dve",
                 "pv_ready", "ao_ready", "at_ready", "at_act", "at_dve", "pool_sum", "pool_mm", "pool_done", "mix_hi", "mix_lo",
                 "q_loaded", "kv_loaded", "poolw_loaded")
        S = [{**both_layers, **{n: sem(f"{n}_{L}") for n in names}} for L in range(DEPTH)]

        block = ctx.enter_context(nc.Block())

        def c_(name, rows=slice(0, P)):
            return cst[rows, CV[name][0]:CV[name][1]]

        def p_(L, name, i=0, n=1):
            return par[:, L, PV[name][0] + i:PV[name][0] + i + n]

        ident, ones = c_("ident"), c_("ones")
        parts = (0, 1)

        def out_parts(L):
            return (0, 1) if L < DEPTH - 1 else (0,)

        def out_tokens(L):
            return T if L < DEPTH - 1 else SEQ

        def block_parts(L, blk):
            return (0, 1) if L < DEPTH - 1 or blk < CTX_BLOCKS else (0,)

        def span(L, blk):
            return SPAN if len(block_parts(L, blk)) > 1 else SEQ

        def ctx_seen(L, blk):
            return 1 + L * IN_PANELS + min(blk + 1, IN_PANELS if L < DEPTH - 1 else CTX_BLOCKS)

        RUN_OUT, RUN_MLP = [1, 2 + FF_GROUPS], [2, 3 + FF_GROUPS]
        NORM_RUN = [0, RUN_OUT[0], RUN_MLP[0] + FF_GROUPS - 1, RUN_OUT[1], RUN_MLP[1] + FF_GROUPS - 1]

        first_panel = [L * LAYER_PANELS for L in range(DEPTH)]
        LAST_PANEL = DEPTH * LAYER_PANELS - 1

        CODES = ((B_KVA, "kva_norm"), (B_QA, "qa_norm"))
        MIX = (B_Z, B_Z + 1, B_Z + 2, B_ATT, B_ATT + 1, B_ATT + 2, B_POOL, B_POOL + 1)
        MIX_ORDER = (0, 1, 2, 6, 7, 3, 4, 5)

        def hb(c):
            return proj[:, B_XS:B_XS + 3, :].rearrange("p b w -> p (b w)")[:, c * INNER:(c + 1) * INNER]

        def swapped_rows(n):
            return (rstd if n else wide[:, 0])[QK_NOPE:QK_DIM, 0:SEQ]

        def at_bank(c):
            return g[c % 2][:, 512 * (c // 2 % 2):512 * (c // 2 % 2) + INNER]

        def value_bank(c):
            return g[0][:, 512 * (c % 2):512 * (c % 2) + INNER]

        BACK = (5, 4, 3, 2, 1)
        FORW = (4, 5, 0, 1, 2, 3)

        def wanted(L):
            return [c for c in FORW if c < XCH or L < DEPTH - 1]

        def units(L):
            return [(h, c) for h in range(HEADS) for c in range(out_tokens(L) // P)]

        def slices(L):
            out = [("back", j, c) for j, c in enumerate(BACK)]
            seen = 0
            for j, c in enumerate(FORW):
                if c in wanted(L):
                    out += [("tiles0", j, c, seen), ("tiles1", j, c, seen), ("sum", j, c, seen), ("gate", j, c, seen)]
                    seen += 1
                else:
                    out.append(("state", j, c))
            return out + [("norm0",), ("norm1",), ("norm2",), ("pool0",), ("pool1",)]

        def slots(L):
            return range(max(len(units(L)) + 1, len(slices(L))))

        def kchunks(c):
            return range(NCH) if c < XCH else range(XCH, NCH)

        def prepares(L, t):
            us = units(L)
            if t < len(us) and us[t][0] + 1 < HEADS and us[t][1] < 2:
                return us[t][0] + 1, us[t][1]
            return None, None

        DTI = {n: i for i, ns in enumerate((("v",), ("mag",), ("e",), ("den",), ("s",), ("s2", "csn"), ("poly", "w"), ("dt",),
                                            ("adt",), ("ecs",))) for n in ns}

        def dv(name):
            return dts[:, DTI[name], :]

        def by_chunk(name):
            return dv(name).rearrange("p (c d h) -> p c d h", c=NCH, d=2)

        def by_dir(name):
            return dv(name).rearrange("p (d c h) -> p d c h", d=2, c=NCH)

        @block.sync
        def _(sp):
            def raw_dma(n, i=0, stride=0):
                sp.wait_ge(lo_ready, n - 1 + stride * i)
                sp.dma_start(w_raw[:, n % 2], panels[bass.ds(n + stride * i, 1)].rearrange("a p k n -> p (a k) n"))\
                  .then_inc(raw_loaded[n % 2], 16)

            def block_dma(q, i=0, stride=0):
                if q > 1:
                    sp.wait_ge(mod_step, q - 1 + stride * i)
                sp.dma_start(mod_rows[:, q % 2], mod_late[bass.ds(q + stride * i, 1)].rearrange("a p k -> p (a k)"))\
                  .then_inc(mod_loaded[q % 2], 16)

            def cond_dma():
                sp.dma_start(cond_b[:], cond_rows).then_inc(cond_loaded, 16)

            def early_dma(b):
                a, z = b * MOD_EARLY // 2, (b + 1) * MOD_EARLY // 2
                sp.dma_start(mod_raw[:, a:z], mod_early[a:z].rearrange("a p k n -> p a k n")).then_inc(early_loaded[b], 16)

            sp.dma_start(cond[:], cond_in).then_inc(cond_loaded, 16)
            cond_dma()
            block_dma(0)
            block_dma(1)
            sp.dma_start(cst[:], consts).then_inc(const_loaded, 16)
            sp.dma_start(msk[:], masks).then_inc(const_loaded, 16)
            sp.dma_start(par[:], params).then_inc(const_loaded, 16)
            sp.dma_start(fin_w[:], final_w).then_inc(const_loaded, 16)
            early_dma(0)
            block_dma(2)
            block_dma(3)
            sp.dma_start(xres[:], x_in).then_inc(x_loaded, 16)
            block_dma(4)
            block_dma(5)
            early_dma(1)
            for q in range(6, MOD_START):
                block_dma(q)
            for n in range(2):
                sp.dma_start(w_raw[:, n], panels[n]).then_inc(raw_loaded[n], 16)
            for n in range(2):
                raw_dma(2 + n)
                block_dma(FIRST_IN + n)
            with sp.Fori(0, (IN_PANELS - 1) // 2 - 1) as i:
                for n in range(2):
                    raw_dma(4 + n, i, 2)
                    block_dma(FIRST_IN + 2 + n, i, 2)
            raw_dma(IN_PANELS + 1)
            block_dma(FIRST_OUT - 2)
            block_dma(FIRST_OUT - 1)
            sp.wait_ge(S[0]["pool_sum"], 2)
            sp.wait_ge(S[0]["gated"], len(wanted(0)))
            cond_dma()
            for j in range(OUT_PANELS):
                raw_dma(IN_PANELS + 2 + j)
                if j < OUT_PANELS - 1:
                    block_dma(FIRST_OUT + 2 * j)
                    block_dma(FIRST_OUT + 2 * j + 1)
            with sp.Fori(0, FF_GROUPS) as i:
                for j in range(2 * KB):
                    raw_dma(IN_PANELS + OUT_PANELS + 2 + j, i, 2 * KB)
                    if j < MOD_PER_GROUP:
                        block_dma(FIRST_MLP + j, i, MOD_PER_GROUP)
            rest = LAYER_PANELS + 2
            with sp.Fori(0, (LAST_PANEL - rest) // 2) as i:
                raw_dma(rest, i, 2)
                raw_dma(rest + 1, i, 2)
            for n in range(rest + (LAST_PANEL - rest) // 2 * 2, LAST_PANEL + 1):
                raw_dma(n)
            for k in range(0, KB, 2):
                sp.wait_ge(norm_hi, 2 * DEPTH * KB + k + 2)
                sp.dma_start(out[:, k:k + 2], xres[:, k:k + 2, 0:SEQ]).then_inc(out_stored, 16)
            sp.wait_ge(out_stored, 16 * KB // 2)

        @block.gpsimd
        def _(pool):
            chain = [0]

            def link(ins):
                chain[0] += 1
                ins.then_inc(pool_chain, 1)
                pool.wait_ge(pool_chain, chain[0])

            def zero_gaps(L):
                if L:
                    pool.wait_ge(panel_used, 1 + first_panel[L])
                for a in (0, XO + SEQ, CO + CTX_LEN):
                    ins = nc.gpsimd.memset(proj[:, :, a:a + GAP], 0.0)
                    ins.then_inc(S[L]["gaps_zero"], 1)

            def pooling(L, b):
                s = S[L]
                blk = B_POOL + b
                lo, hi = XO, XO + span(L, blk)
                end = hi + GAP
                pool.wait_ge(s["gaps_zero"], 3)
                pool.wait_ge(psum_free, 1 + first_panel[L] + IN_PANELS)
                pool.wait_ge(ctx_free, ctx_seen(L, blk))
                pool.wait_ge(mod_step, (FIRST_OUT if L == 0 else FIRST_MLP + MOD_PANELS))
                u = proj[:, blk, :]
                link(nc.gpsimd.tensor_tensor(pool_a[:, 1:end], u[:, 0:end - 1], u[:, 1:end], ALU.add))
                link(nc.gpsimd.tensor_tensor(pool_b[:, 2:end - 1], pool_a[:, 1:end - 2], pool_a[:, 3:end], ALU.add))
                if b == 1:
                    link(nc.gpsimd.tensor_tensor(pool_a[:, 4:end - 3], pool_b[:, 2:end - 5], pool_b[:, 6:end - 1], ALU.add))
                    link(nc.gpsimd.tensor_tensor(pool_b[HD:P, lo:hi], pool_a[HD:P, lo - 4:hi - 4],
                                                 pool_a[HD:P, lo + 4:hi + 4], ALU.add))
                for rows, w in ((slice(0, HD), pool_a), (slice(HD, P), pool_b)):
                    link(nc.gpsimd.tensor_scalar(w[rows, lo:hi], w[rows, lo:hi], cst[rows, CV["rw"][0] + b:CV["rw"][0] + b + 1],
                                                 None, ALU.mult))
                    for part in block_parts(L, blk):
                        _, (a, z) = part_columns(part)
                        for a0, e0 in ((a, 0), (z - 8, 8)):
                            e = CV["edge"][0] + 16 * b + e0
                            link(nc.gpsimd.tensor_tensor(w[rows, a0:a0 + 8], w[rows, a0:a0 + 8], cst[rows, e:e + 8], ALU.mult))
                        link(nc.gpsimd.tensor_tensor(u[rows, a:z], w[rows, a:z], u[rows, a:z], ALU.subtract))
                pool.sem_inc(s["pool_sum"], 1)

            def norm_ctx(v):
                a, z = SEQ, T
                pool.wait_ge(rstd_ready, v + 1)

                def scale(k):
                    if k >= 2:
                        pool.wait_ge(ctx_lo, KB * v + k - 1)
                    nc.gpsimd.tensor_tensor(tmp[:, k % 2, a:z], xres[:, k, a:z], rstd[:, a:z], ALU.mult).then_inc(ctx_scaled, 1)

                scale(0)
                for k in range(KB):
                    if k + 1 < KB:
                        scale(k + 1)
                    pool.wait_ge(norm_hi, KB * v + k + 1)
                    nc.gpsimd.tensor_tensor(act_lo[:, k, a:z], tmp[:, k % 2, a:z], act_hi[:, k, a:z].bitcast(F32), ALU.subtract)\
                        .then_inc(ctx_lo, 1)

            def query_weights(L):
                pool.wait_ge(panel_used, 1 + first_panel[L] + IN_PANELS)
                pool.dma_start(wqb[:], wqb_in[L]).then_inc(S[L]["q_loaded"], 16)

            def other_weights(L):
                if L:
                    pool.wait_ge(S[L - 1]["k_ready"], HEADS)
                    pool.wait_ge(S[L - 1]["v_ready"], before(L - 1, "v_ready") + NCH)
                    pool.wait_ge(S[L - 1]["pool_mm"], 2)
                pool.dma_start(wkvb[:], wkvb_in[L]).then_inc(S[L]["kv_loaded"], 16)
                pool.dma_start(poolw[:], poolw_in[L]).then_inc(S[L]["poolw_loaded"], 16)

            def ropes(L):
                s = S[L]
                R = slice(QK_NOPE, QK_DIM)
                for h in range(-1, HEADS):
                    rows = proj[R, B_MISC, XO:XO + SEQ] if h < 0 else qT[R, h % 2, 0:SEQ]
                    pool.wait_ge(s["swapped"], h + 2)
                    swapped = swapped_rows(h + 1)
                    link(nc.gpsimd.tensor_tensor(swapped, swapped, c_("sin", R), ALU.mult))
                    link(nc.gpsimd.tensor_tensor(rows, rows, c_("cos", R), ALU.mult))
                    link(nc.gpsimd.tensor_tensor(rows, rows, swapped, ALU.add))
                    pool.sem_inc(s["kr_done" if h < 0 else "rope_done"], 1)
                    if 0 <= h < 2:
                        pooling(L, h)

            for L in range(DEPTH):
                zero_gaps(L)
                if L == 0:
                    pool.wait_ge(const_loaded, 64)
                norm_ctx(2 * L)
                other_weights(L)
                query_weights(L)
                ropes(L)
                if L < DEPTH - 1:
                    norm_ctx(2 * L + 1)

        @block.scalar
        def _(act):
            A = nc.scalar.activation
            chain = [0]

            def link(ins):
                chain[0] += 1
                ins.then_inc(act_chain, 1)
                act.wait_ge(act_chain, chain[0])

            def hi_part(n, i=0, stride=0):
                act.wait_ge(raw_loaded[n % 2], 16 * (n // 2 + 1) + 8 * stride * i)
                if n > 1 or stride:
                    act.wait_ge(panel_used, 1 + n - 1 + stride * i)
                A(w_hi[:, n % 2], w_raw[:, n % 2], ACT.Copy).then_inc(hi_ready, 1)

            def square(run, m, W, n=None, i=0, stride=0):
                if n is not None:
                    act.wait_ge(psum_free, 1 + n + 1 + stride * i)
                if m >= 3:
                    act.wait_ge(sq_added, (KB - 1) * run + m - 2 + (KB - 1) * i)
                A(rstd[:, 0:W] if m == 0 else sq[:, m % 2, 0:W], xres[:, m, 0:W], ACT.Square).then_inc(sq_ready, 1)

            def norm_rstd(v, W):
                nc.scalar.preload_act_table_set("natural_log_exp_and_others")
                act.wait_ge(sum_ready, v + 1)
                link(A(rstd[:, 0:W], m01[:, 0:W], ACT.Ln, bias=eps[:], scale=1.0 / D_MODEL))
                A(rstd[:, 0:W], rstd[:, 0:W], ACT.Exp, scale=-0.5).then_inc(rstd_ready, 1)

            def norm_apply(v, L, which):
                shift = (SH1 if which == 1 else SH2) * KB
                ps = parts if (which == 1 or L < DEPTH - 1) else (0,)
                for k in range(KB):
                    bias = modv[:, L, shift + k, :]
                    act.wait_ge(scaled, KB * v + k + 1)
                    ins = A(act_hi[:, k, 0:SEQ], tmp[:, k % 2, 0:SEQ], ACT.Identity, bias=bias[:, 0:1])
                    if len(ps) > 1:
                        act.wait_ge(ctx_scaled, KB * v + k + 1)
                        t = tmp[:, k % 2, SEQ:T]
                        A(act_hi[:, k, SEQ:T], t, ACT.Identity, scale=gain[:, k, 1:2], bias=bias[:, 1:2])
                        ins = A(t, t, ACT.Identity, scale=gain[:, k, 1:2], bias=bias[:, 1:2])
                    ins.then_inc(norm_hi, 1)

            def evacuate_in(n, blk, i=0, stride=0):
                act.wait_ge(panel_used, 1 + n + 1 + stride * i)
                A(proj[:, bass.ds(blk + stride * i, 1), XO:XO + SEQ] if stride else proj[:, blk, XO:XO + SEQ],
                  g[n % 2][:, 0:SEQ], ACT.Copy).then_inc(psum_free, 1)

            def conv_first(L, b):
                s = S[L]
                act.wait_ge(ctx_free, ctx_seen(L, B_XS + b))
                act.wait_ge(psum_free, 1 + first_panel[L] + B_XS + b + 1)
                to = XO + span(L, B_XS + b)
                act.wait_ge(s["gaps_zero"], 3)
                if b >= 2:
                    act.wait_ge(s["conv_done"], b - 1)
                A(wide[:, b % 2, XO:to], proj[:, B_XS + b, XO:to], ACT.Identity, scale=p_(L, "conv_w", 7 + b),
                  bias=p_(L, "conv_b", b)).then_inc(s["conv_pre"], 1)

            def conv_last(L, b):
                s = S[L]
                act.wait_ge(s["conv_acc"], before(L, "conv_acc") + b + 1)
                to = XO + span(L, B_XS + b)
                A(proj[:, B_XS + b, XO:to], wide[:, b % 2, XO:to], ACT.Silu).then_inc(s["conv_done"], 1)

            def code_squares(L, j):
                s = S[L]
                b0 = CODES[j][0]
                if j:
                    act.wait_ge(s["csum_ready"], before(L, "csum_ready") + 1)
                for b in range(2):
                    act.wait_ge(ctx_free, ctx_seen(L, b0 + b))
                    act.wait_ge(psum_free, 1 + first_panel[L] + b0 + b + 1)
                    for part in block_parts(L, b0):
                        (a, z), (pa, pz) = part_columns(part)
                        ins = A(sq[:, b, a:z], proj[:, b0 + b, pa:pz], ACT.Square)
                ins.then_inc(s["csq_ready"], 1)

            def code_rstd(L, j):
                s = S[L]
                act.wait_ge(s["csum_ready"], before(L, "csum_ready") + j + 1)
                if j:
                    act.wait_ge(s["code_ready"], 1)
                W = T if len(block_parts(L, CODES[j][0])) > 1 else SEQ
                nc.scalar.preload_act_table_set("natural_log_exp_and_others")
                link(A(rstd[:, 0:W], m01[:, 0:W], ACT.Ln, bias=eps[:], scale=1.0 / LORA))
                A(rstd[:, 0:W], rstd[:, 0:W], ACT.Exp, scale=-0.5).then_inc(s["crstd_ready"], 1)

            def copy_tok(L, c):
                act.wait_ge(S[L]["tok_tp"], before(L, "tok_tp") + c + 1)
                A(tok[:, c, :], m01[:, 0:5 * P], ACT.Copy).then_inc(S[L]["tok_ready"], 1)

            def gate_values(L, b):
                act.wait_ge(psum_free, 1 + first_panel[L] + B_Z + b + 1)
                act.wait_ge(ctx_free, ctx_seen(L, B_Z + b))
                to = XO + span(L, B_Z + b)
                A(proj[:, B_Z + b, XO:to], proj[:, B_Z + b, XO:to], ACT.Silu).then_inc(S[L]["z_done"], 1)

            def input_tail(L, j):
                if j == 8:
                    code_squares(L, 0)
                if j == 12:
                    code_squares(L, 1)
                if j < 15:
                    conv_first(L, j - 8)
                if 9 <= j < 16:
                    conv_last(L, j - 9)
                if j in (9, 13):
                    code_rstd(L, (j - 9) // 4)
                if j == 15:
                    gate_values(L, 0)
                    gate_values(L, 1)
                if j == 16:
                    gate_values(L, 2)
                if j >= 15:
                    copy_tok(L, j - 15)

            def mixer(L):
                s = S[L]
                n_out = out_tokens(L)
                first = first_panel[L]
                nc.scalar.preload_act_table_set("natural_log_exp_and_others")
                act.wait_ge(s["dt_pre"], before(L, "dt_pre") + 1)
                link(A(dv("mag"), dv("v"), ACT.Abs))
                A(dv("e"), dv("mag"), ACT.Exp, scale=-1.0).then_inc(s["dt_exp"], 1)
                A(a_exp[:, L, :], p_(L, "a_log", 0, 12), ACT.Exp).then_inc(s["dt_exp"], 1)

                def copy_swapped(n, src):
                    if n > 1:
                        act.wait_ge(s["rope_done"], n - 1)
                    A(swapped_rows(n), src, ACT.Copy).then_inc(s["swapped"], 1)

                def copy_value(c):
                    act.wait_ge(s["v_ready"], before(L, "v_ready") + c + 1)
                    A(vtok[:, c, :], value_bank(c), ACT.Copy).then_inc(s["v_done"], 1)

                nq = n_out // P

                def prepare(h, stage):
                    if stage == 0:
                        act.wait_ge(s["q_ready"], h + 1)
                        if h >= 2:
                            act.wait_ge(s["s_ready"], nq * (h - 1))
                        A(qT[0:QK_DIM, h % 2, 0:n_out], g[1][0:QK_DIM, 0:n_out], ACT.Copy)
                        copy_swapped(h + 1, g[1][QK_DIM:P, 0:SEQ])
                    else:
                        act.wait_ge(s["k_ready"], h + 1)
                        A(kT[0:QK_NOPE, h % 2, 0:T], g[1][0:QK_NOPE, 0:T], ACT.Copy).then_inc(s["k_copied"], 1)

                act.wait_ge(s["code_ready"], 2)
                copy_swapped(0, proj[QK_DIM:P, B_MISC, XO:XO + SEQ])
                copy_tok(L, 2)
                prepare(0, 0)
                for c in range(3, NCH):
                    copy_tok(L, c)
                    copy_value(c - 3)
                    if c == 3:
                        prepare(0, 1)
                act.wait_ge(s["cs_neg"], before(L, "cs_neg") + 1)
                A(by_dir("ecs"), pd[:, 128:200].rearrange("p (d c h) -> p d c h", d=2, c=NCH), ACT.Exp).then_inc(s["cs_exp"], 1)
                A(dv("mag"), pd[:, 200:272], ACT.Exp).then_inc(s["cs_exp"], 1)
                A(dv("e"), dv("w"), ACT.Exp).then_inc(s["cs_exp"], 1)
                for c in range(3, NCH):
                    copy_value(c)
                act.wait_ge(s["kr_done"], 1)
                for j in range(2):
                    for part in parts:
                        (a, z), (pa, pz) = part_columns(part)
                        ins = A(kT[QK_NOPE:QK_DIM, j, a:z], proj[QK_NOPE:QK_DIM, B_MISC, pa:pz], ACT.Copy)
                ins.then_inc(s["kr_rows"], 1)
                us = units(L)
                sl = slices(L)

                def tiles(c, seen, gr):
                    for d in range(2):
                        t = 4 * seen + 2 * gr + d
                        act.wait_ge(s["r_ready"], t + 1)
                        if t >= 2:
                            act.wait_ge(s["m_ready"], t - 1)
                        if t >= 4 and t % 4 == 0:
                            act.wait_ge(s["ytok_ready"], seen)
                        for hh in range(GH):
                            h = GH * gr + hh
                            ins = A(E[:, d, hh * P:(hh + 1) * P], m01[:, 512 * d + hh * P:512 * d + (hh + 1) * P], ACT.Exp,
                                    bias=by_dir("csn")[:, d, c, h:h + 1])
                        ins.then_inc(s["e_ready"], 1)

                def group_rstd(n):
                    act.wait_ge(s["gsum_ready"], n + 1)
                    if n:
                        act.wait_ge(s["ssd_done"], 1)
                    else:
                        act.wait_ge(s["rope_done"], HEADS)
                    link(A(rstd[:, 0:n_out], (m01, pair)[n][:, 0:n_out], ACT.Ln, bias=eps[:], scale=1.0 / GW))
                    A(rstd[:, 0:n_out], rstd[:, 0:n_out], ACT.Exp, scale=-0.5).then_inc(s["grstd_ready"], 1)

                def square(slot, b):
                    to = XO + span(L, B_Z + b)
                    return A(wide[:, slot, XO:to], proj[:, B_Z + b, XO:to], ACT.Square)

                def slice_work(kind, *x):
                    if kind == "tiles0":
                        tiles(x[1], x[2], 0)
                    elif kind == "tiles1":
                        tiles(x[1], x[2], 1)
                    elif kind == "norm0":
                        act.wait_ge(s["gated"], len(wanted(L)))
                        square(0, 0)
                        square(1, 1).then_inc(s["gsq_ready"], 1)
                    elif kind == "norm1":
                        act.wait_ge(s["gsum_ready"], 1)
                        square(0, 2).then_inc(s["gsq_ready"], 1)
                        group_rstd(0)
                    elif kind == "norm2":
                        group_rstd(1)
                    elif kind in ("pool0", "pool1"):
                        b = int(kind[4:])
                        act.wait_ge(s["pool_mm"], b + 1)
                        for part in out_parts(L):
                            (a, z), (pa, pz) = part_columns(part)
                            ins = A(proj[:, B_POOL + b, pa:pz], m01[:, a:z], ACT.Copy, scale=p_(L, "pool_scale", b))
                        ins.then_inc(s["pool_done"], 1)

                for t in slots(L):
                    if 1 <= t <= len(us):
                        act.wait_ge(s["pt_ready"], t)
                        if t >= 2:
                            act.wait_ge(s["pv_ready"], t - 1)
                        A(PT[:, XCH:NCH, :], g[1][:, SEQ:T], ACT.Copy).then_inc(s["pt_act"], 1)
                    if t < len(us):
                        lo = 0 if us[t][1] < XCH else SEQ
                        act.wait_ge(s["max_ready"], t + 1)
                        if t >= 2:
                            act.wait_ge(s["pt_ready"], t - 1)
                        A(Pm[:, t % 2, lo:T], g[0][:, lo:T], ACT.Exp, bias=sm[:, t % 2, 0:1], scale=float(QK_DIM) ** -0.5,
                          accum_out=sm[:, t % 2, 1:2]).then_inc(s["p_ready"], 1)
                    for work in sl[t:t + 1]:
                        slice_work(*work)
                    h, stage = prepares(L, t)
                    if h is not None:
                        prepare(h, stage)

                def mix_hi(k):
                    for part in out_parts(L):
                        (a, z), (pa, pz) = part_columns(part)
                        ins = A(act_hi[:, k, a:z], proj[:, MIX[k], pa:pz], ACT.Copy)
                    ins.then_inc(s["mix_hi"], 1)

                if L == 0:
                    act.wait_ge(cond_loaded, 48)
                    A(cond_b[:], cond_b[:], ACT.Silu).then_inc(cond_ready, 1)
                act.wait_ge(s["pv_ready"], len(us))
                act.wait_ge(s["ssd_done"], 2)
                act.wait_ge(s["pool_done"], 2)
                mix_hi(MIX_ORDER[0])
                for c in range(0, nq, 2):
                    act.wait_ge(s["at_ready"], c + 1)
                    A(proj[:, B_ATT:B_ATT + 3, chunk_at(c):chunk_at(c) + P], at_bank(c).rearrange("p (b t) -> p b t", b=3),
                      ACT.Copy).then_inc(s["at_act"], 1)
                for k in MIX_ORDER[1:5]:
                    mix_hi(k)
                act.wait_ge(s["at_act"], (nq + 1) // 2)
                act.wait_ge(s["at_dve"], nq // 2)
                for k in MIX_ORDER[5:]:
                    mix_hi(k)

            def mlp(L):
                n_out = out_tokens(L)
                n0 = first_panel[L] + IN_PANELS + OUT_PANELS
                S2 = 2 * KB
                hid = L * FF_GROUPS * KB

                def group(i, ex, last):
                    for j in range(KB):
                        act.wait_ge(panel_used, 1 + n0 + j + 1 + ex + S2 * i)
                        A(tmp[:, j % 2, 0:n_out], g[(n0 + j) % 2][:, 0:n_out], ACT.Relu).then_inc(relu_ready, 1)
                        act.wait_ge(hid_ready, hid + j + 1 + ex // 2 + KB * i)
                        A(h_hi[:, j, 0:n_out], sq[:, j % 2, 0:n_out], ACT.Copy).then_inc(hid_hi, 1)
                        hi_part(n0 + j + 2 + ex, i, S2)
                    run, out = RUN_MLP[L] + ex // S2, n0 + KB + ex
                    for j in range(KB):
                        if j:
                            square(run, j - 1, n_out, out + j - 1, i, S2)
                        if not (last and j >= KB - 2):
                            hi_part(out + j + 2, i, S2)
                    square(run, KB - 1, n_out, out + KB - 1, i, S2)

                if L < DEPTH - 1:
                    with act.Fori(0, FF_GROUPS) as i:
                        group(i, 0, False)
                else:
                    with act.Fori(0, FF_GROUPS - 1) as i:
                        group(i, 0, False)
                    group(0, S2 * (FF_GROUPS - 1), True)

            act.wait_ge(cond_loaded, 32)
            A(cond[:], cond[:], ACT.Silu).then_inc(cond_ready, 1)
            A(cond_b[:], cond_b[:], ACT.Silu).then_inc(cond_ready, 1)
            nc.scalar.preload_act_table_set("natural_log_exp_and_others")
            act.wait_ge(x_loaded, 16)
            act.wait_ge(cond_ready, 3)
            for m in range(KB):
                square(0, m, T)
            hi_part(0)
            hi_part(1)
            for L in range(DEPTH):
                first = first_panel[L]
                norm_rstd(2 * L, T)
                norm_apply(2 * L, L, 1)
                with act.Fori(0, CTX_BLOCKS // 4) as i:
                    for j in range(4):
                        evacuate_in(first + j, j, i, 4)
                        hi_part(first + j + 2, i, 4)
                for j in range(CTX_BLOCKS, IN_PANELS):
                    input_tail(L, j)
                    evacuate_in(first + j, j)
                    hi_part(first + j + 2)
                mixer(L)
                for j in range(OUT_PANELS):
                    if j:
                        square(RUN_OUT[L], j - 1, out_tokens(L), first + IN_PANELS + j - 1)
                    hi_part(first + IN_PANELS + j + 2)
                square(RUN_OUT[L], KB - 1, out_tokens(L), first + IN_PANELS + KB - 1)
                norm_rstd(2 * L + 1, out_tokens(L))
                norm_apply(2 * L + 1, L, 2)
                mlp(L)
            norm_rstd(2 * DEPTH, SEQ)

        @block.vector
        def _(dve):
            TT, TS, STT = nc.vector.tensor_tensor, nc.vector.tensor_scalar, nc.vector.scalar_tensor_tensor
            chain = [0]

            def link(ins):
                chain[0] += 1
                ins.then_inc(dve_chain, 1)
                dve.wait_ge(dve_chain, chain[0])

            def lo_part(n, i=0, stride=0):
                dve.wait_ge(hi_ready, n + 1 + stride * i)
                TT(w_lo[:, n % 2], w_raw[:, n % 2], w_hi[:, n % 2].bitcast(F32), ALU.subtract).then_inc(lo_ready, 1)

            def modulation(L, seg0, seg1, used):
                dve.wait_ge(mod_step, used)
                dve.wait_ge(const_loaded, 64)
                for seg in range(seg0, seg1):
                    a, z = seg * KB, (seg + 1) * KB
                    products = modv[:, L, a:z, :]
                    if L == 0 and seg == SC1:
                        dve.wait_ge(mod_used, MOD_EARLY)
                        products = g[1][:, 0:2 * KB].rearrange("p (m c) -> p m c", c=2)
                    link(TT(modv[:, L, a:z, :], products,
                            p_(L, "mod_b", a, z - a).rearrange("p (m c) -> p m c", c=1).broadcast_to([P, z - a, 2]), ALU.add))

            def make_gain(L, which):
                seg = (SC1 if which == 1 else SC2) * KB
                w = p_(L, "norm1" if which == 1 else "norm2", 0, KB).rearrange("p (m c) -> p m c", c=1).broadcast_to([P, KB, 2])
                link(STT(out=gain[:], in0=modv[:, L, seg:seg + KB, :], scalar=1.0, in1=w, op0=ALU.add, op1=ALU.mult))

            def add_square(run, m, W, i=0):
                if m == 0:
                    return
                dve.wait_ge(sq_ready, KB * run + m + 1 + KB * i)
                if m >= 2:
                    dve.wait_ge(sq_added, (KB - 1) * run + m - 1 + (KB - 1) * i)
                TT(rstd[:, 0:W], rstd[:, 0:W], sq[:, m % 2, 0:W], ALU.add).then_inc(sq_added, 1)

            def norm(v, L, which):
                shift = (SH1 if which == 1 else SH2) * KB
                dve.wait_ge(rstd_ready, v + 1)

                def scale(k):
                    if k >= 2:
                        dve.wait_ge(norm_lo, KB * v + k - 1)
                    STT(out=tmp[:, k % 2, 0:SEQ], in0=xres[:, k, 0:SEQ], scalar=gain[:, k, 0:1], in1=rstd[:, 0:SEQ],
                        op0=ALU.mult, op1=ALU.mult).then_inc(scaled, 1)

                scale(0)
                for k in range(KB):
                    if k + 1 < KB:
                        scale(k + 1)
                    dve.wait_ge(norm_hi, KB * v + k + 1)
                    STT(out=act_lo[:, k, 0:SEQ], in0=tmp[:, k % 2, 0:SEQ], scalar=modv[:, L, shift + k, 0:1],
                        in1=act_hi[:, k, 0:SEQ].bitcast(F32), op0=ALU.add, op1=ALU.subtract).then_inc(norm_lo, 1)

            def evacuate_in(n, blk, L, i=0, stride=0):
                dve.wait_ge(panel_used, 1 + n + 1 + stride * i)
                nc.vector.tensor_copy(
                    proj[:, bass.ds(blk + stride * i, 1), CO:CO + CTX_LEN] if stride else proj[:, blk, CO:CO + CTX_LEN],
                    g[n % 2][:, SEQ:T]).then_inc(ctx_free, 1)

            def conv_taps(L, b):
                s = S[L]
                dve.wait_ge(s["conv_pre"], before(L, "conv_pre") + b + 1)
                n = span(L, B_XS + b)
                w = wide[:, b % 2, XO:XO + n]
                for tap, shift in ((0, -1), (2, 1), (3, 2)):
                    ins = STT(out=w, in0=proj[:, B_XS + b, XO + shift:XO + shift + n], scalar=p_(L, "conv_w", 7 * tap + b),
                              in1=w, op0=ALU.mult, op1=ALU.add)
                    if tap < 3:
                        link(ins)
                ins.then_inc(s["conv_acc"], 1)

            def small(L):
                s = S[L]
                dve.wait_ge(s["dt_tp"], before(L, "dt_tp") + 1)
                link(TT(by_chunk("v").rearrange("p c d h -> p c (d h)"), pd[:, 0:DTN].rearrange("p (c j) -> p c j", c=NCH),
                        p_(L, "dt_bias", 0, 12).rearrange("p (c j) -> p c j", c=1).broadcast_to([P, NCH, 12]), ALU.add))
                dve.sem_inc(s["dt_pre"], 1)
                dve.wait_ge(s["dt_exp"], before(L, "dt_exp") + 2)
                link(TS(dv("den"), dv("e"), 2.0, None, ALU.add))
                link(nc.vector.reciprocal(dv("den"), dv("den")))
                link(TT(dv("s"), dv("e"), dv("den"), ALU.mult))
                link(TT(dv("s2"), dv("s"), dv("s"), ALU.mult))
                link(TS(dv("poly"), dv("s2"), 1.0 / 15, None, ALU.mult))
                for odd in (13, 11, 9, 7, 5, 3):
                    link(STT(out=dv("poly"), in0=dv("poly"), scalar=1.0 / odd, in1=dv("s2"), op0=ALU.add, op1=ALU.mult))
                link(STT(out=dv("poly"), in0=dv("poly"), scalar=1.0, in1=dv("s"), op0=ALU.add, op1=ALU.mult))
                link(TS(dv("v"), dv("v"), 0.0, None, ALU.max))
                link(STT(out=dv("dt"), in0=dv("poly"), scalar=2.0, in1=dv("v"), op0=ALU.mult, op1=ALU.add))
                STT(out=dv("adt").rearrange("p (c j) -> p c j", c=NCH), in0=dv("dt").rearrange("p (c j) -> p c j", c=NCH),
                    scalar=-1.0, in1=a_exp[:, L, :].rearrange("p (c j) -> p c j", c=1).broadcast_to([P, NCH, 12]),
                    op0=ALU.mult, op1=ALU.mult).then_inc(s["adt_ready"], 1)
                dve.wait_ge(s["cs_ready"], before(L, "cs_ready") + 1)
                link(TS(dv("csn"), pd[:, 128:200], -1.0, None, ALU.mult))
                for d in range(2):
                    ins = TT(by_dir("w")[:, d], pd[:, 200:272].rearrange("p (c d h) -> p d c h", c=NCH, d=2)[:, d],
                             by_dir("csn")[:, d], ALU.add)
                ins.then_inc(s["cs_neg"], 1)
                dve.wait_ge(s["cs_exp"], before(L, "cs_exp") + 3)
                for d in range(2):
                    link(TT(by_dir("w")[:, d], by_dir("e")[:, d], by_chunk("dt").rearrange("p c d h -> p d c h")[:, d], ALU.mult))

            def per_head(ap):
                return ap.rearrange("p (h j) -> p h j", j=1).broadcast_to([P, HEADS, HD])

            def by_head(ap):
                return ap.rearrange("p (h j) -> p h j", j=HD)

            def weigh(L, n):
                s = S[L]
                if n == len(BACK) + NCH - 1:
                    return
                c, d = (BACK[n], 1) if n < len(BACK) else (FORW[n - len(BACK)], 0)
                if n:
                    dve.wait_ge(s["st_ready"], n)
                TT(by_head(xw[:]), by_head(tok[:, c, 0:INNER]), per_head(by_dir("w")[:, d, c, :]), ALU.mult)\
                    .then_inc(s["xw_ready"], 1)

            def code_norm(L, j):
                s = S[L]
                b0, w = CODES[j]
                dve.wait_ge(s["crstd_ready"], j + 1)
                for b in range(2):
                    for part in block_parts(L, b0):
                        (a, z), (pa, pz) = part_columns(part)
                        ins = STT(out=proj[:, b0 + b, pa:pz], in0=proj[:, b0 + b, pa:pz], scalar=p_(L, w, b),
                                  in1=rstd[:, a:z], op0=ALU.mult, op1=ALU.mult)
                ins.then_inc(s["code_ready"], 1)

            def mixer(L):
                s = S[L]
                n_out = out_tokens(L)
                small(L)
                dve.wait_ge(s["tok_ready"], NCH)
                weigh(L, 0)
                us = units(L)
                sl = slices(L)

                def tiles(c, seen, gr):
                    dve.wait_ge(s["cb_ready"], seen + 1)
                    if seen:
                        dve.wait_ge(s["m_used"], seen)
                    for d in range(2):
                        dve.wait_ge(s["e_ready"], 4 * seen + 2 * gr + d + 1)
                        for hh in range(GH):
                            h = GH * gr + hh
                            ins = STT(out=M[:, gr, d, hh * P:(hh + 1) * P], in0=E[:, d, hh * P:(hh + 1) * P],
                                      scalar=by_chunk("dt")[:, c, d, h:h + 1], in1=pd[:, gr * P:(gr + 1) * P],
                                      op0=ALU.mult, op1=ALU.mult)
                        ins.then_inc(s["m_ready"], 1)

                def forward(j, c):
                    dve.wait_ge(s["st_ready"], len(BACK) + j + 1)
                    if j == 0:
                        link(nc.vector.tensor_copy(hf[:], pd[:, 0:INNER]))
                    else:
                        link(TT(by_head(hf[:]), by_head(hf[:]), per_head(by_chunk("mag")[:, c, 0, :]), ALU.mult))
                        link(TT(hf[:], hf[:], pd[:, 0:INNER], ALU.add))
                    dve.sem_inc(s["hf_ready"], 1)
                    weigh(L, len(BACK) + j + 1)

                low, high, every = slice(0, HD), slice(HD, P), slice(0, P)

                def group_norm(n):
                    dve.wait_ge(s["grstd_ready"], n + 1)
                    for b, rows in ((0, every), (1, low)) if n == 0 else ((1, high), (2, every)):
                        for part in out_parts(L):
                            (a, z), (pa, pz) = part_columns(part)
                            ins = STT(out=proj[rows, B_Z + b, pa:pz], in0=proj[rows, B_Z + b, pa:pz],
                                      scalar=p_(L, "ssd_norm", b)[rows], in1=rstd[rows, a:z], op0=ALU.mult, op1=ALU.mult)
                    ins.then_inc(s["ssd_done"], 1)

                def slice_work(kind, *x):
                    if kind == "back":
                        j, c = x
                        dve.wait_ge(s["st_ready"], j + 1)
                        src = (pd, pmod)[j % 2][:, 0:INNER]
                        if j == 0:
                            link(nc.vector.tensor_copy(hb(c - 1), src))
                        else:
                            link(TT(by_head(hb(c - 1)), by_head(hb(c)), per_head(by_chunk("mag")[:, c, 1, :]), ALU.mult))
                            link(TT(hb(c - 1), hb(c - 1), src, ALU.add))
                        dve.sem_inc(s["hb_ready"], 1)
                        weigh(L, j + 1)
                    elif kind == "state":
                        forward(*x)
                    elif kind == "tiles0":
                        tiles(x[1], x[2], 0)
                    elif kind == "tiles1":
                        tiles(x[1], x[2], 1)
                    elif kind == "sum":
                        j, c, seen = x
                        y = ytok[:]
                        if seen:
                            dve.wait_ge(s["yt_ready"], seen)
                        link(TT(by_head(y), by_head(tok[:, c, 0:INNER]), per_head(p_(L, "ssd_d", 0, HEADS)), ALU.mult))
                        dve.wait_ge(s["yoff_ready"], seen + 1)
                        for d in range(2):
                            if (d == 0 and j > 0) or (d == 1 and c < NCH - 1):
                                link(TT(by_head(E[:, d, :]), by_head(m01[:, 512 * d:512 * d + INNER]),
                                        per_head(by_dir("ecs")[:, d, c, :]), ALU.mult))
                                link(TT(y, y, E[:, d, :], ALU.add))
                    elif kind == "gate":
                        j, c, seen = x
                        if j < NCH - 1:
                            forward(j, c)
                    elif kind in ("norm0", "norm1"):
                        n = int(kind[4:])
                        rows = (low, high)[n]
                        to = XO + span(L, B_Z)
                        dve.wait_ge(s["gsq_ready"], n + 1)
                        TT(wide[rows, 0, XO:to], wide[rows, 0, XO:to], wide[rows, 1, XO:to], ALU.add).then_inc(s["gsq_added"], 1)

                def slice_end(kind, *x):
                    if kind in ("tiles0", "tiles1"):
                        seen, gr = x[2], int(kind[5:])
                        dve.wait_ge(s["m_ready"], 4 * seen + 2 * gr + 2)
                        TT(M[:, gr, 0], M[:, gr, 0], M[:, gr, 1], ALU.add).then_inc(s["m_sum"], 1)
                    elif kind == "sum":
                        dve.wait_ge(s["m_used"], x[2] + 1)
                        TT(ytok[:], ytok[:], pmod[:, 0:INNER], ALU.add).then_inc(s["ytok_ready"], 1)
                    elif kind in ("norm1", "norm2"):
                        group_norm(int(kind[4:]) - 1)
                    elif kind == "gate":
                        j, c, seen = x
                        dve.wait_ge(s["yt_ready"], seen + 1)
                        dve.wait_ge(s["z_done"], before(L, "z_done") + 3)
                        zz = proj[:, B_Z:B_Z + 3, chunk_at(c):chunk_at(c) + P]
                        TT(zz, pmod[:, 0:3 * P].rearrange("p (b t) -> p b t", b=3), zz, ALU.mult).then_inc(s["gated"], 1)

                for t in slots(L):
                    if t < len(us):
                        lo = 0 if us[t][1] < XCH else SEQ
                        dve.wait_ge(s["s_ready"], t + 1)
                        link(nc.vector.tensor_reduce(sm[:, t % 2, 2:3], g[0][:, lo:T], AX.X, ALU.max))
                        TS(sm[:, t % 2, 0:1], sm[:, t % 2, 2:3], -float(QK_DIM) ** -0.5, None, ALU.mult).then_inc(s["max_ready"], 1)
                    if 1 <= t <= len(us):
                        h, c = us[t - 1]
                        dve.wait_ge(s["pt_ready"], t)
                        if t >= 2:
                            dve.wait_ge(s["pv_ready"], t - 1)
                        if c < XCH:
                            nc.vector.tensor_copy(PT[:, 0:XCH, :], g[1][:, 0:SEQ]).then_inc(s["pt_dve"], 1)
                        else:
                            dve.sem_inc(s["pt_dve"], 1)
                        link(nc.vector.reciprocal(sm[:, (t - 1) % 2, 3:4], sm[:, (t - 1) % 2, 1:2]))
                    for work in sl[t:t + 1]:
                        slice_work(*work)
                    if 1 <= t <= len(us):
                        dve.wait_ge(s["pv_ready"], t)
                        TS(ao[:, c, h * V_HEAD:(h + 1) * V_HEAD], g[1][:, T:T + V_HEAD], sm[:, (t - 1) % 2, 3:4], None, ALU.mult)\
                            .then_inc(s["ao_ready"], 1)
                    for work in sl[t:t + 1]:
                        slice_end(*work)
                nq = n_out // P
                for c in range(1, nq, 2):
                    dve.wait_ge(s["at_ready"], c + 1)
                    nc.vector.tensor_copy(proj[:, B_ATT:B_ATT + 3, chunk_at(c):chunk_at(c) + P],
                                          at_bank(c).rearrange("p (b t) -> p b t", b=3)).then_inc(s["at_dve"], 1)
                dve.wait_ge(s["at_ready"], nq)
                for n, k in enumerate(MIX_ORDER):
                    dve.wait_ge(s["mix_hi"], n + 1)
                    for part in out_parts(L):
                        (a, z), (pa, pz) = part_columns(part)
                        ins = TT(act_lo[:, k, a:z], proj[:, MIX[k], pa:pz], act_hi[:, k, a:z].bitcast(F32), ALU.subtract)
                    ins.then_inc(s["mix_lo"], 1)

            def block_product(q, i=0, stride=0):
                if q:
                    dve.wait_ge(mod_step, q + stride * i)
                dve.wait_ge(mod_loaded[q % 2], 16 * (q // 2 + 1) + 8 * stride * i)
                layer = int(q >= FIRST_MLP)
                m = q if q < FIRST_IN else q + KB if q < FIRST_MLP else q - FIRST_MLP
                for v in range(2):
                    total = modv[:, layer, bass.ds(m + stride * i, 1), v] if stride else modv[:, layer, m:m + 1, v]
                    ins = STT(out=mod_rows[:, q % 2] if v else pair[:], in0=mod_rows[:, q % 2], scalar=1.0, in1=cond_b[:, v],
                              op0=ALU.mult, op1=ALU.mult, accum_out=total)
                ins.then_inc(mod_step, 1)

            def add_gated(L, n, gate, m, i=0, stride=0):
                dve.wait_ge(panel_used, 1 + n + 1 + stride * i)
                for part in out_parts(L):
                    (a, z), _ = part_columns(part)
                    ins = STT(out=xres[:, m, a:z], in0=g[n % 2][:, a:z], scalar=modv[:, L, gate * KB + m, part:part + 1],
                              in1=xres[:, m, a:z], op0=ALU.mult, op1=ALU.add)
                ins.then_inc(psum_free, 1)

            def mlp(L):
                n_out = out_tokens(L)
                n0 = first_panel[L] + IN_PANELS + OUT_PANELS
                S2 = 2 * KB
                hid = L * FF_GROUPS * KB

                def group(i, ex, last):
                    for j in range(KB):
                        if L == 0:
                            block_product(FIRST_MLP + j, i, MOD_PER_GROUP)
                        m = hid + j + ex // 2
                        dve.wait_ge(relu_ready, m + 1 + KB * i)
                        STT(out=sq[:, j % 2, 0:n_out], in0=g[(n0 + j) % 2][:, 0:n_out], scalar=0.0, in1=tmp[:, j % 2, 0:n_out],
                            op0=ALU.max, op1=ALU.mult).then_inc(hid_ready, 1)
                        dve.wait_ge(hid_ready, m + 1 + KB * i)
                        dve.sem_inc(psum_free, 1)
                        dve.wait_ge(hid_hi, m + 1 + KB * i)
                        TT(h_lo[:, j, 0:n_out], sq[:, j % 2, 0:n_out], h_hi[:, j, 0:n_out].bitcast(F32), ALU.subtract)\
                            .then_inc(hid_lo, 1)
                        lo_part(n0 + j + 2 + ex, i, S2)
                    run = RUN_MLP[L] + ex // S2
                    for j in range(KB):
                        if L == 0 and KB + j < MOD_PER_GROUP:
                            block_product(FIRST_MLP + KB + j, i, MOD_PER_GROUP)
                        if j:
                            add_square(run, j - 1, n_out, i)
                        add_gated(L, n0 + KB + j + ex, G2, j, i, S2)
                        if not (last and j >= KB - 2):
                            lo_part(n0 + KB + j + 2 + ex, i, S2)
                    add_square(run, KB - 1, n_out, i)

                if L < DEPTH - 1:
                    with dve.Fori(0, FF_GROUPS) as i:
                        group(i, 0, False)
                else:
                    with dve.Fori(0, FF_GROUPS - 1) as i:
                        group(i, 0, False)
                    group(0, S2 * (FF_GROUPS - 1), True)

            dve.sem_inc(panel_used, 1)
            dve.sem_inc(psum_free, 1)
            dve.sem_inc(ctx_free, 1)
            nc.vector.memset(eps[:], EPS).then_inc(cond_ready, 1)
            dve.wait_ge(cond_ready, 3)
            for q in range(MOD_START - 2):
                block_product(q)
            for m in range(KB):
                add_square(0, m, T)
            for q in range(MOD_START - 2, MOD_START):
                block_product(q)
            lo_part(0)
            lo_part(1)
            for L in range(DEPTH):
                first = first_panel[L]
                if L == 0:
                    modulation(0, 0, 2, FIRST_IN)
                else:
                    modulation(L, 0, 6, FIRST_MLP + MOD_PANELS)
                dve.sem_inc(mod_ready, 1)
                make_gain(L, 1)
                norm(2 * L, L, 1)
                with dve.Fori(0, CTX_BLOCKS // 4) as i:
                    for j in range(4):
                        if L == 0:
                            block_product(FIRST_IN + j, i, 4)
                        evacuate_in(first + j, j, L, i, 4)
                        lo_part(first + j + 2, i, 4)
                for j in range(CTX_BLOCKS, IN_PANELS):
                    if L == 0:
                        block_product(FIRST_IN + j)
                        if j == IN_PANELS - 1:
                            block_product(FIRST_OUT - 1)
                    if j < 15:
                        conv_taps(L, j - 8)
                    if j in (10, 14):
                        code_norm(L, (j - 10) // 4)
                    if len(block_parts(L, j)) > 1:
                        evacuate_in(first + j, j, L)
                    lo_part(first + j + 2)
                if L == 0:
                    modulation(0, 2, 4, FIRST_OUT)
                    dve.sem_inc(mod_ready, 1)
                mixer(L)
                if L == 0:
                    dve.wait_ge(cond_ready, 4)
                for j in range(OUT_PANELS):
                    if L == 0 and j < OUT_PANELS - 1:
                        block_product(FIRST_OUT + 2 * j)
                        block_product(FIRST_OUT + 2 * j + 1)
                    if j:
                        add_square(RUN_OUT[L], j - 1, out_tokens(L))
                    add_gated(L, first + IN_PANELS + j, G1, j)
                    lo_part(first + IN_PANELS + j + 2)
                add_square(RUN_OUT[L], KB - 1, out_tokens(L))
                if L == 0:
                    modulation(0, 4, 6, FIRST_MLP)
                    dve.sem_inc(mod_ready, 1)
                make_gain(L, 2)
                norm(2 * L + 1, L, 2)
                mlp(L)
            dve.wait_ge(rstd_ready, 2 * DEPTH + 1)
            for k in range(KB):
                STT(out=xres[:, k, 0:SEQ], in0=xres[:, k, 0:SEQ], scalar=fin_w[:, k:k + 1], in1=rstd[:, 0:SEQ],
                    op0=ALU.mult, op1=ALU.mult).then_inc(norm_hi, 1)

        @block.tensor
        def _(pe):
            mm = nc.tensor.matmul

            def begin(n, free_ctx, i=0, stride=0):
                pe.wait_ge(lo_ready, n + 1 + stride * i)
                if n > 1 or stride:
                    pe.wait_ge(psum_free, 1 + max(n - 1, 0) + stride * i)
                    if free_ctx is not None:
                        pe.wait_ge(ctx_free, free_ctx + stride * i)

            def products(n, m, k, rhs, want_ctx):
                s = n % 2
                rhs_hi, rhs_lo = rhs
                for term, (w, r) in enumerate(((w_hi, rhs_hi), (w_hi, rhs_lo), (w_lo, rhs_hi))):
                    st, sp_ = m == 0 and term == 0, m == KB - 1 and term == 2
                    ins = mm(g[s][:, 0:SEQ], w[:, s, k, :], r[:, k, 0:SEQ], start=st, stop=sp_)
                    if want_ctx:
                        ins = mm(g[s][:, SEQ:T], w[:, s, k, :], r[:, k, SEQ:T], start=st, stop=sp_)
                return ins

            act_split, hid_split = (act_hi, act_lo), (h_hi, h_lo)

            def panel(n, rhs, want_ctx, free_ctx=None, ready=None, i=0, stride=0):
                begin(n, free_ctx, i, stride)
                for k in range(KB):
                    if ready is not None:
                        ready(k)
                    ins = products(n, k, k, rhs, want_ctx)
                ins.then_inc(panel_used, 1)

            def two_panels(n, rhs, want_ctx, ready, free_ctx=(None, None), i=0, stride=0, order=range(KB)):
                begin(n, free_ctx[0], i, stride)
                for m, k in enumerate(order):
                    ready(m)
                    ins = products(n, m, k, rhs, want_ctx)
                    if m == 1:
                        begin(n + 1, free_ctx[1], i, stride)
                    if 1 <= m <= KB // 2:
                        products(n + 1, m - 1, order[m - 1], rhs, want_ctx)
                ins.then_inc(panel_used, 1)
                for m in range(KB // 2, KB):
                    ins = products(n + 1, m, order[m], rhs, want_ctx)
                ins.then_inc(panel_used, 1)

            def early_mod(q):
                for k in range(KB):
                    ins = mm(g[1][:, 2 * q:2 * q + 2], mod_raw[:, q, k, :], cond[:, k, :], start=(k == 0), stop=(k == KB - 1))
                ins.then_inc(mod_used, 1)

            def norm_sums(v):
                W = T if v < 2 * DEPTH - 1 else SEQ
                pe.wait_ge(sq_added, (KB - 1) * (NORM_RUN[v] + 1))
                for a, z in ((0, SEQ), (SEQ, T)) if W > SEQ else ((0, SEQ),):
                    ins = mm(m01[:, a:z], ones, rstd[:, a:z], start=True, stop=True)
                ins.then_inc(sum_ready, 1)

            def code_sums(L, j):
                s = S[L]
                pe.wait_ge(s["csq_ready"], before(L, "csq_ready") + j + 1)
                if j:
                    pe.wait_ge(s["crstd_ready"], 1)
                for part in block_parts(L, CODES[j][0]):
                    (a, z), _ = part_columns(part)
                    for b in range(2):
                        ins = mm(m01[:, a:z], ones, sq[:, b, a:z], start=(b == 0), stop=(b == 1))
                ins.then_inc(s["csum_ready"], 1)

            def turn_chunk(L, c):
                s = S[L]
                pe.wait_ge(s["conv_done"], 5)
                if c:
                    pe.wait_ge(s["tok_ready"], c)
                else:
                    pe.wait_ge(s["crstd_ready"], 2)
                for b in range(5):
                    ins = nc.tensor.transpose(m01[:, b * P:(b + 1) * P], proj[:, B_XS + b, chunk_at(c):chunk_at(c) + P], ident)
                ins.then_inc(s["tok_tp"], 1)

            def mixer(L):
                s = S[L]
                n_out = out_tokens(L)
                first = first_panel[L]
                pe.wait_ge(psum_free, 1 + first + IN_PANELS)
                pe.wait_ge(ctx_free, ctx_seen(L, NBLK - 1))
                for c in range(NCH):
                    ins = nc.tensor.transpose(pd[:, 12 * c:12 * c + 12], proj[0:12, B_MISC, chunk_at(c):chunk_at(c) + P],
                                              ident[0:12, 0:12])
                ins.then_inc(s["dt_tp"], 1)
                def value(c):
                    if c >= 2:
                        pe.wait_ge(s["v_done"], c - 1)
                    for k in range(2):
                        ins = mm(value_bank(c), proj[:, B_KVA + k, chunk_at(c):chunk_at(c) + P],
                                 wkvb[:, k, :].rearrange("p (h j) -> p h j", j=P)[:, :, QK_NOPE:P], start=(k == 0), stop=(k == 1))
                    ins.then_inc(s["v_ready"], 1)

                def prepare(h, stage, read=None):
                    if stage == 0:
                        for part in out_parts(L):
                            (a, z), (pa, pz) = part_columns(part)
                            if part and read:
                                pe.wait_ge(s["ao_ready"], read)
                            for k in range(2):
                                ins = mm(g[1][:, a:z], wqb[:, k, h * P:(h + 1) * P], proj[:, B_QA + k, pa:pz],
                                         start=(k == 0), stop=(k == 1))
                        ins.then_inc(s["q_ready"], 1)
                    else:
                        pe.wait_ge(s["swapped"], h + 2)
                        for part in parts:
                            (a, z), (pa, pz) = part_columns(part)
                            if part and read:
                                pe.wait_ge(s["ao_ready"], read)
                            for k in range(2):
                                ins = mm(g[1][0:QK_NOPE, a:z], wkvb[:, k, h * P:h * P + QK_NOPE], proj[:, B_KVA + k, pa:pz],
                                         start=(k == 0), stop=(k == 1))
                        ins.then_inc(s["k_ready"], 1)

                pe.wait_ge(s["code_ready"], 2)
                pe.wait_ge(s["q_loaded"], 16)
                prepare(0, 0)
                pe.wait_ge(s["kv_loaded"], 16)
                for c in range(3, NCH):
                    turn_chunk(L, c)
                    value(c - 3)
                    if c == 3:
                        prepare(0, 1)
                pe.wait_ge(s["adt_ready"], before(L, "adt_ready") + 1)
                adt = by_chunk("adt")
                mm(pd[:, 128:164], c_("from"), adt[:, :, 0, :], start=True, stop=True)
                mm(pd[:, 164:200], c_("upto"), adt[:, :, 1, :], start=True, stop=True)
                mm(pd[:, 200:272], ones, dv("adt"), start=True, stop=True).then_inc(s["cs_ready"], 1)
                for c in range(3, NCH):
                    value(c)

                def bank_free(h, stage):
                    if stage == 0:
                        pe.wait_ge(s["swapped"], h + 2)
                    else:
                        pe.wait_ge(s["k_copied"], h + 1)

                def state(c, n, dst):
                    pe.wait_ge(s["xw_ready"], n + 1)
                    for gr in range(GROUPS):
                        ins = mm(dst[:, gr * GW:(gr + 1) * GW], tok[:, c, INNER + gr * P:INNER + (gr + 1) * P],
                                 xw[:, gr * GW:(gr + 1) * GW], start=True, stop=True)
                    ins.then_inc(s["st_ready"], 1)

                def tiles(c, seen, gr):
                    for d in range(2):
                        t = 4 * seen + 2 * gr + d
                        if t >= 2:
                            pe.wait_ge(s["e_ready"], t - 1)
                        for hh in range(GH):
                            h = GH * gr + hh
                            o = m01[:, 512 * d + hh * P:512 * d + (hh + 1) * P]
                            mm(o, adt[:, c, d, h:h + 1].broadcast_to([P, P]), c_("from") if d == 0 else c_("upto"),
                               start=True, stop=False)
                            ins = mm(o, msk[:, 2, :], msk[:, d, :], start=False, stop=True)
                        ins.then_inc(s["r_ready"], 1)

                def group_sums(n):
                    pe.wait_ge(s["gsq_added"], n + 1)
                    for part in out_parts(L):
                        (a, z), (pa, pz) = part_columns(part)
                        ins = mm((m01, pair)[n][:, a:z], ones, wide[:, 0, pa:pz], start=True, stop=True)
                    ins.then_inc(s["gsum_ready"], 1)

                def slice_work(kind, *x):
                    if kind == "back":
                        j, c = x
                        if j >= 2:
                            pe.wait_ge(s["hb_ready"], j - 1)
                        state(c, j, (pd, pmod)[j % 2])
                    elif kind == "state":
                        j, c = x
                        if j:
                            pe.wait_ge(s["hf_ready"], j)
                        else:
                            pe.wait_ge(s["hb_ready"], len(BACK))
                        state(c, len(BACK) + j, pd)
                    elif kind == "tiles0":
                        j, c, seen = x
                        if j:
                            pe.wait_ge(s["hf_ready"], j)
                        pe.wait_ge(s["hb_ready"], len(BACK))
                        cols = slice(chunk_at(c), chunk_at(c) + P)
                        for gr in range(GROUPS):
                            ins = mm(pd[:, gr * P:(gr + 1) * P], proj[:, B_B + gr, cols], proj[:, B_C + gr, cols], start=True, stop=True)
                        ins.then_inc(s["cb_ready"], 1)
                        if seen:
                            pe.wait_ge(s["ytok_ready"], seen)
                        tiles(c, seen, 0)
                    elif kind == "tiles1":
                        tiles(x[1], x[2], 1)
                    elif kind == "sum":
                        j, c, seen = x
                        cols = slice(chunk_at(c), chunk_at(c) + P)
                        pe.wait_ge(s["e_ready"], 4 * seen + 4)
                        for d in range(2):
                            if (d == 0 and j > 0) or (d == 1 and c < NCH - 1):
                                h = hf[:] if d == 0 else hb(c)
                                for gr in range(GROUPS):
                                    ins = mm(m01[:, 512 * d + gr * GW:512 * d + (gr + 1) * GW], proj[:, B_C + gr, cols],
                                             h[:, gr * GW:(gr + 1) * GW], start=True, stop=True)
                        ins.then_inc(s["yoff_ready"], 1)
                        pe.wait_ge(s["m_sum"], 2 * seen + 2)
                        if seen:
                            pe.wait_ge(s["gated"], seen)
                        for h in range(HEADS):
                            ins = mm(pmod[:, h * HD:(h + 1) * HD], M[:, h // GH, 0, (h % GH) * P:(h % GH + 1) * P],
                                     tok[:, c, h * HD:(h + 1) * HD], start=True, stop=True)
                        ins.then_inc(s["m_used"], 1)
                    elif kind == "gate":
                        j, c, seen = x
                        if j < NCH - 1:
                            state(c, len(BACK) + j, pd)

                def slice_end(kind, *x):
                    if kind == "gate":
                        j, c, seen = x
                        pe.wait_ge(s["ytok_ready"], seen + 1)
                        for b in range(3):
                            ins = nc.tensor.transpose(pmod[:, b * P:(b + 1) * P], ytok[:, b * P:(b + 1) * P], ident)
                        ins.then_inc(s["yt_ready"], 1)
                    elif kind in ("norm0", "norm1"):
                        group_sums(int(kind[4:]))
                    elif kind in ("pool0", "pool1"):
                        b = int(kind[4:])
                        pe.wait_ge(s["pool_sum"], b + 1)
                        pe.wait_ge(s["poolw_loaded"], 16)
                        if b:
                            pe.wait_ge(s["pool_done"], 1)
                        else:
                            pe.wait_ge(s["grstd_ready"], 1)
                        for part in out_parts(L):
                            (a, z), (pa, pz) = part_columns(part)
                            ins = mm(m01[:, a:z], poolw[:, b, :], proj[:, B_POOL + b, pa:pz], start=True, stop=True)
                        ins.then_inc(s["pool_mm"], 1)

                pe.wait_ge(s["v_done"], NCH)
                pe.wait_ge(s["kr_rows"], 1)
                bank_free(0, 1)
                us = units(L)
                sl = slices(L)
                nq = n_out // P
                for t in slots(L):
                    if t < len(us):
                        h, c = us[t]
                        if t:
                            pe.wait_ge(s["p_ready"], t)
                        pe.wait_ge(s["rope_done"], h + 1)
                        pe.wait_ge(s["k_copied"], h + 1)
                        for a, z in ((0, SEQ), (SEQ, T)) if c < XCH else ((SEQ, T),):
                            ins = mm(g[0][:, a:z], qT[0:QK_DIM, h % 2, c * P:(c + 1) * P], kT[0:QK_DIM, h % 2, a:z],
                                     start=True, stop=True)
                        ins.then_inc(s["s_ready"], 1)
                    if 1 <= t <= len(us):
                        h, c = us[t - 1]
                        pe.wait_ge(s["p_ready"], t)
                        if t >= 2:
                            pe.wait_ge(s["ao_ready"], t - 1)
                        if prepares(L, t - 1)[0] is not None:
                            bank_free(*prepares(L, t - 1))
                        for kc in kchunks(c):
                            ins = nc.tensor.transpose(g[1][:, kc * P:(kc + 1) * P], Pm[:, (t - 1) % 2, kc * P:(kc + 1) * P], ident)
                        ins.then_inc(s["pt_ready"], 1)
                    for work in sl[t:t + 1]:
                        slice_work(*work)
                    if 1 <= t <= len(us):
                        h, c = us[t - 1]
                        pe.wait_ge(s["pt_act"], t)
                        pe.wait_ge(s["pt_dve"], t)
                        for kc in kchunks(c):
                            ins = mm(g[1][:, T:T + V_HEAD], PT[:, kc, :], vtok[:, kc, h * V_HEAD:(h + 1) * V_HEAD],
                                     start=(kc == kchunks(c)[0]), stop=(kc == NCH - 1))
                        ins.then_inc(s["pv_ready"], 1)
                    for work in sl[t:t + 1]:
                        slice_end(*work)
                    if prepares(L, t)[0] is not None:
                        prepare(*prepares(L, t), t)
                pe.wait_ge(s["ao_ready"], len(us))
                for c in range(nq):
                    if c >= 4:
                        pe.wait_ge(s["at_dve" if c % 2 else "at_act"], c // 2 - 1)
                    for b in range(3):
                        ins = nc.tensor.transpose(at_bank(c)[:, b * P:(b + 1) * P], ao[:, c, b * P:(b + 1) * P], ident)
                    ins.then_inc(s["at_ready"], 1)
                pe.wait_ge(s["at_act"], (nq + 1) // 2)
                pe.wait_ge(s["at_dve"], nq // 2)

            def norm_block(v):
                def ready(k):
                    pe.wait_ge(norm_lo, KB * v + k + 1)
                    if v < 2 * DEPTH - 1:
                        pe.wait_ge(ctx_lo, KB * v + k + 1)
                return ready

            def mix_block(L):
                def ready(k):
                    pe.wait_ge(S[L]["mix_lo"], k + 1)
                return ready

            pe.wait_ge(const_loaded, 64)
            pe.wait_ge(cond_ready, 3)
            for b in range(2):
                pe.wait_ge(early_loaded[b], 16)
                for q in range(b * MOD_EARLY // 2, (b + 1) * MOD_EARLY // 2):
                    early_mod(q)
            for L in range(DEPTH):
                first = first_panel[L]
                both = L < DEPTH - 1
                in0, out0, n0 = first, first + IN_PANELS, first + IN_PANELS + OUT_PANELS
                norm_sums(2 * L)

                def in_ctx(j):
                    return 1 + L * IN_PANELS + max(j - 1, 0)

                with pe.Fori(0, CTX_BLOCKS // 4) as i:
                    two_panels(in0, act_split, True, norm_block(2 * L), (in_ctx(0), in_ctx(1)), i, 4)
                    for j in range(2, 4):
                        panel(in0 + j, act_split, True, in_ctx(j), None, i, 4)
                for j in range(CTX_BLOCKS, IN_PANELS):
                    panel(in0 + j, act_split, both, in_ctx(j) if both else None)
                    if j in (8, 12):
                        code_sums(L, (j - 8) // 4)
                    if j >= 14:
                        turn_chunk(L, j - 14)
                pe.wait_ge(mod_ready, 2 + 2 * L)
                mixer(L)
                two_panels(out0, act_split, both, mix_block(L), order=MIX_ORDER)
                for j in range(2, OUT_PANELS):
                    panel(out0 + j, act_split, both)
                norm_sums(2 * L + 1)
                with pe.Fori(0, FF_GROUPS) as i:
                    def hidden(k):
                        pe.wait_ge(hid_lo, L * FF_GROUPS * KB + k + 1 + KB * i)

                    two_panels(n0, act_split, both, norm_block(2 * L + 1), i=i, stride=2 * KB)
                    for j in range(2, 2 * KB):
                        if j < KB:
                            panel(n0 + j, act_split, both, i=i, stride=2 * KB)
                        else:
                            panel(n0 + j, hid_split, both, ready=hidden if j == KB else None, i=i, stride=2 * KB)
            norm_sums(2 * DEPTH)


def kernel(**inputs):
    import numpy as np
    import concourse.bacc as bacc
    from concourse.bass_utils import run_bass_kernel_spmd

    a = {k: np.asarray(v) for k, v in inputs.items()}
    f32 = np.float32

    def blocks(w):
        w = w.reshape(w.shape[:-1] + (w.shape[-1] // P, P))
        return np.moveaxis(w, -1, 0)

    def panel_stack(w):
        n = w.shape[1] // P
        return w.reshape(KB, P, n, P).transpose(2, 1, 0, 3)

    pairs = QK_ROPE // 4
    f = np.arange(QK_ROPE)
    half = f // pairs % 2
    partner = np.where(half == 0, f + pairs, f - pairs)
    off_dt = 2 * INNER + 2 * GROUPS * STATE
    off_qa = off_dt + 2 * HEADS
    off_rope = off_qa + 2 * LORA
    off_pool = off_rope + QK_ROPE
    stack = []
    for L in range(DEPTH):
        w = a["w_in"][L]
        misc = np.zeros((D_MODEL, P), f32)
        misc[:, 0:2 * HEADS] = w[:, off_dt:off_qa]
        misc[:, QK_NOPE:QK_DIM] = w[:, off_rope:off_pool]
        misc[:, QK_DIM:P] = w[:, off_rope + partner]
        w = np.concatenate([misc, w[:, off_qa + LORA:off_rope], w[:, INNER:off_dt], w[:, off_qa:off_qa + LORA],
                            w[:, 0:INNER], w[:, off_pool:]], axis=1)
        stack += [panel_stack(w), panel_stack(a["w_out"][L])]
        for j in range(FF_GROUPS):
            stack += [panel_stack(a["w_mlp1"][L][:, j * D_MODEL:(j + 1) * D_MODEL]),
                      panel_stack(a["w_mlp2"][L][j * D_MODEL:(j + 1) * D_MODEL])]
    panels = np.ascontiguousarray(np.concatenate(stack))
    mod_early = panel_stack(a["mod_w"][0][:, D_MODEL:2 * D_MODEL])
    rows = a["mod_w"].transpose(0, 2, 1).reshape(DEPTH, MOD_PANELS, P, D_MODEL)
    mod_late = np.concatenate([rows[0, 0:KB], rows[0, 2 * KB:], rows[1]])

    params = np.zeros((P, DEPTH, NPV), f32)
    for L in range(DEPTH):
        def put(name, v):
            params[:, L, PV[name][0]:PV[name][1]] = v
        put("mod_b", blocks(a["mod_b"][L]))
        put("norm1", blocks(a["norm1_w"][L]))
        put("norm2", blocks(a["norm2_w"][L]))
        put("conv_w", blocks(a["conv_w"][L]).reshape(P, -1))
        put("conv_b", blocks(a["conv_b"][L]))
        put("ssd_norm", blocks(a["ssd_norm_w"][L]))
        put("qa_norm", blocks(a["q_a_norm_w"][L]))
        put("kva_norm", blocks(a["kv_a_norm_w"][L]))
        put("pool_scale", blocks(a["pool_scale"][L]))
        put("dt_bias", a["dt_bias"][L].reshape(1, -1))
        put("a_log", a["a_log"][L].reshape(1, -1))
        put("ssd_d", a["ssd_d"][L].reshape(1, -1))

    consts = np.zeros((P, NCV), f32)

    def const(name, v, rows=slice(0, P)):
        consts[rows, CV[name][0]:CV[name][1]] = v
    i = np.arange(P)
    const("ident", np.eye(P))
    const("from", i[:, None] <= i[None, :])
    const("upto", i[:, None] >= i[None, :])
    const("ones", 1.0)
    t = np.arange(SEQ)
    grid_w = 64
    inv = (f32(10000.0) ** (-np.arange(pairs, dtype=f32) / f32(pairs))).astype(f32)
    pos = np.stack([t // grid_w, t % grid_w]).astype(f32)
    ang = (pos[f // (2 * pairs)] * inv[f % pairs][:, None]).astype(f32)
    const("cos", np.cos(ang), slice(QK_NOPE, QK_DIM))
    const("sin", np.where(half[:, None] == 0, -np.sin(ang), np.sin(ang)), slice(QK_NOPE, QK_DIM))
    for b in range(2):
        for r in range(2):
            w = 2 << (2 * b + r)
            rows = slice(HD * r, HD * (r + 1))
            consts[rows, CV["rw"][0] + b] = 1.0 / w
            e = CV["edge"][0] + 16 * b
            for q in range(8):
                consts[rows, e + q] = w / (min(q, w // 2) + w // 2)
                consts[rows, e + 8 + q] = w / (w // 2 + min(8 - q, w // 2))
    import ml_dtypes
    masks = np.zeros((P, 3, P), ml_dtypes.bfloat16)
    masks[:, 0] = np.where(i[:, None] <= i[None, :], 0.0, -1e30)
    masks[:, 1] = np.where(i[:, None] >= i[None, :], 0.0, -1e30)
    masks[:, 2] = np.eye(P)

    poolw = np.zeros((DEPTH, P, 2, P), f32)
    for b in range(2):
        for r in range(2):
            poolw[:, HD * r:HD * (r + 1), b, HD * r:HD * (r + 1)] = a["pool_w"][:, 2 * b + r]
    tokens = np.concatenate([a["x"][0], a["ctx"][0]]).reshape(T, KB, P).transpose(2, 1, 0)
    cond = np.stack([a["c"][0], a["c_ctx"]]).reshape(2, KB, P).transpose(2, 1, 0)

    cond_rows = np.broadcast_to(np.stack([a["c"][0], a["c_ctx"]]).reshape(1, 2, D_MODEL), (P, 2, D_MODEL))

    wqb = a["w_q_b"].reshape(DEPTH, LORA, HEADS, QK_DIM)
    wqb = np.concatenate([wqb, wqb[..., QK_NOPE + partner]], axis=3).reshape(DEPTH, LORA, HEADS * P)

    def lora(w):
        return w.reshape(DEPTH, 2, P, w.shape[-1]).transpose(0, 2, 1, 3)

    arrays = {"panels": panels, "mod_early": mod_early, "mod_late": mod_late, "tokens": tokens, "cond": cond,
              "cond_rows": cond_rows, "params": params,
              "final_w": blocks(a["final_norm_w"]), "consts": consts, "masks": masks, "wqb": lora(wqb),
              "wkvb": lora(a["w_kv_b"]), "poolw": poolw}
    nc = bacc.Bacc("TRN2", target_bir_lowering=False, num_devices=1)
    args = []
    for name in arrays:
        arrays[name] = np.ascontiguousarray(arrays[name])
        args.append(nc.dram_tensor(name, arrays[name].shape, mybir.dt.from_np(arrays[name].dtype), kind="ExternalInput").ap())
    args.append(nc.dram_tensor("out", (P, KB, SEQ), F32, kind="ExternalOutput").ap())
    build(nc, *args)
    r = run_bass_kernel_spmd(nc, [arrays], core_ids=[0])
    return r.results[0]["out"].transpose(2, 1, 0).reshape(1, SEQ, D_MODEL)
```
